# Optimizing a Trainium2 kernel written in Bass

```python
import math
import jax, jax.numpy as jnp
from jax import lax
import numpy as np

D_MODEL = 1024
BATCH = 1
SEQ = 128
DEPTH = 2
DEC_BATCH = 1
DEC_SEQ = 512
PAST_LEN = 128

GRID_W = 64
HEAD_DIM = 64
N_Q_HEADS = 8
N_KV_HEADS = 2
Q_PER_KV = N_Q_HEADS // N_KV_HEADS
ATTN_WIDTH = N_Q_HEADS * HEAD_DIM
KV_WIDTH = N_KV_HEADS * HEAD_DIM
WINDOW = 128
BLOCK = 128
ROPE_BASE = 10000.0
ROT_AXIS = HEAD_DIM // 2
SG_GROUPS = 8
SG_CHUNK = 128
SG_WIDTH = D_MODEL - ATTN_WIDTH
SG_GROUP_DIM = SG_WIDTH // SG_GROUPS
IN_WIDTH = ATTN_WIDTH + 2 * KV_WIDTH + 2 * SG_WIDTH
SPLITS = (ATTN_WIDTH, ATTN_WIDTH + KV_WIDTH, ATTN_WIDTH + 2 * KV_WIDTH,
          ATTN_WIDTH + 2 * KV_WIDTH + SG_WIDTH)
PEER_HEADS = 8
PEER_KEYS = 128
PEER_EXPERTS = PEER_KEYS * PEER_KEYS
PEER_QDIM = 256
PEER_HALF = PEER_QDIM // 2
PEER_TOPK = 16
TOKEN_BLOCK = 128
LN_EPS = 1e-5
NEG_INF = -1e30
DEEPNORM_ALPHA = (2.0 * DEPTH) ** 0.25
DEEPNORM_BETA = (8.0 * DEPTH) ** -0.25

kernel_name = 'hymba_gmlp_swa_peer_deepnorm_step'

def layer_norm(x, g, b):
    xf = x.astype(jnp.float32)
    mu = jnp.mean(xf, axis=-1, keepdims=True)
    var = jnp.mean(jnp.square(xf - mu), axis=-1, keepdims=True)
    return ((xf - mu) * lax.rsqrt(var + LN_EPS) * g.astype(jnp.float32)
            + b.astype(jnp.float32)).astype(x.dtype)

def modulation(cond, w_mod, b_mod):
    m = jax.nn.silu(cond) @ w_mod + b_mod
    return jnp.split(m[..., None, :], 6, axis=-1)

def axial_rope(n_tokens):
    rows = n_tokens // GRID_W
    row = jnp.repeat(jnp.arange(rows), GRID_W).astype(jnp.float32)
    col = jnp.tile(jnp.arange(GRID_W), rows).astype(jnp.float32)
    inv_freq = 1.0 / (ROPE_BASE ** (jnp.arange(0, ROT_AXIS, 2, dtype=jnp.float32) / ROT_AXIS))
    ang_r = row[:, None] * inv_freq[None, :]
    ang_c = col[:, None] * inv_freq[None, :]
    return (jnp.cos(ang_r), jnp.sin(ang_r), jnp.cos(ang_c), jnp.sin(ang_c))

def _rotate(xh, cos, sin):
    x1, x2 = jnp.split(xh, 2, axis=-1)
    cos = cos[:, None, :]
    sin = sin[:, None, :]
    return jnp.concatenate([x1 * cos - x2 * sin, x1 * sin + x2 * cos], axis=-1)

def apply_axial_rope(x, rope):
    cr, sr, cc, sc = rope
    xf = x.astype(jnp.float32)
    out = jnp.concatenate([_rotate(xf[..., :ROT_AXIS], cr, sr),
                           _rotate(xf[..., ROT_AXIS:], cc, sc)], axis=-1)
    return out.astype(x.dtype)

def project_heads(h, w_in):
    B, T = h.shape[0], h.shape[1]
    p = h @ w_in
    q, k, v, su, sv = jnp.split(p, SPLITS, axis=-1)
    q = q.reshape(B, T, N_Q_HEADS, HEAD_DIM)
    k = k.reshape(B, T, N_KV_HEADS, HEAD_DIM)
    v = v.reshape(B, T, N_KV_HEADS, HEAD_DIM)
    return q, k, v, jax.nn.gelu(su), jax.nn.gelu(sv)

def sink_probs(logits, sink):
    s = jnp.broadcast_to(sink.astype(jnp.float32)[:, :, None, None], logits.shape[:-1] + (1,))
    p = jax.nn.softmax(jnp.concatenate([s, logits], axis=-1), axis=-1)
    return p[..., 1:]

def context_attention(q, k, v, sink):
    B, S = q.shape[0], q.shape[1]
    nb = S // BLOCK
    scale = HEAD_DIM ** -0.5
    qb = q.reshape(B, nb, BLOCK, N_KV_HEADS, Q_PER_KV, HEAD_DIM).transpose(1, 0, 2, 3, 4, 5)

    def one_block(qi):
        logits = jnp.einsum('bqkgd,bskd->bkgqs', qi, k).astype(jnp.float32) * scale
        p = sink_probs(logits, sink)
        return jnp.einsum('bkgqs,bskd->bqkgd', p.astype(v.dtype), v)

    o = lax.map(one_block, qb)
    return o.transpose(1, 0, 2, 3, 4, 5).reshape(B, S, ATTN_WIDTH)

def latent_attention(q, k, v, k_ctx, v_ctx, sink):
    B, T = q.shape[0], q.shape[1]
    nb = T // BLOCK
    scale = HEAD_DIM ** -0.5
    qb = q.reshape(B, nb, BLOCK, N_KV_HEADS, Q_PER_KV, HEAD_DIM)

    def band(x):
        xp = jnp.pad(x, ((0, 0), (BLOCK, BLOCK), (0, 0), (0, 0)))
        xp = xp.reshape(B, nb + 2, BLOCK, N_KV_HEADS, HEAD_DIM)
        return jnp.concatenate([xp[:, :-2], xp[:, 1:-1], xp[:, 2:]], axis=2)

    kb, vb = band(k), band(v)
    qpos = jnp.arange(nb)[:, None] * BLOCK + jnp.arange(BLOCK)[None, :]
    kpos = jnp.arange(nb)[:, None] * BLOCK - BLOCK + jnp.arange(3 * BLOCK)[None, :]
    mask = ((jnp.abs(qpos[:, :, None] - kpos[:, None, :]) <= WINDOW)
            & (kpos[:, None, :] >= 0) & (kpos[:, None, :] < T))
    lb = jnp.einsum('bnqkgd,bnjkd->bnkgqj', qb, kb).astype(jnp.float32) * scale
    lb = jnp.where(mask[None, :, None, None], lb, NEG_INF)
    lc = jnp.einsum('bnqkgd,blkd->bnkgql', qb, k_ctx).astype(jnp.float32) * scale
    p = sink_probs(jnp.concatenate([lb, lc], axis=-1), sink)
    pb = p[..., :3 * BLOCK].astype(v.dtype)
    pc = p[..., 3 * BLOCK:].astype(v.dtype)
    o = (jnp.einsum('bnkgqj,bnjkd->bnqkgd', pb, vb)
         + jnp.einsum('bnkgql,blkd->bnqkgd', pc, v_ctx))
    return o.reshape(B, T, ATTN_WIDTH)

def spatial_gating(u, v, ln_g, ln_b, w_s, b_s):
    B, T = u.shape[0], u.shape[1]
    v = layer_norm(v, ln_g, ln_b)
    vc = v.reshape(B, T // SG_CHUNK, SG_CHUNK, SG_GROUPS, SG_GROUP_DIM)
    s = jnp.einsum('gpq,bnqgc->bnpgc', w_s, vc) + b_s.T[:, :, None]
    return u * s.reshape(B, T, SG_WIDTH)

def peer(h, w_q, key1, key2, u_tab, v_tab):
    B, T, D = h.shape
    n = B * T
    x = h.reshape(n, D)
    q = (x @ w_q).reshape(n, PEER_HEADS, 2, PEER_HALF).astype(jnp.float32)
    s1 = jnp.einsum('nhd,kd->nhk', q[:, :, 0], key1.astype(jnp.float32))
    s2 = jnp.einsum('nhd,kd->nhk', q[:, :, 1], key2.astype(jnp.float32))
    t1, i1 = lax.top_k(s1, PEER_TOPK)
    t2, i2 = lax.top_k(s2, PEER_TOPK)
    cand = (t1[..., :, None] + t2[..., None, :]).reshape(n, PEER_HEADS, PEER_TOPK * PEER_TOPK)
    cand_idx = (i1[..., :, None] * PEER_KEYS + i2[..., None, :]).reshape(n, PEER_HEADS, PEER_TOPK * PEER_TOPK)
    top, pos = lax.top_k(cand, PEER_TOPK)
    idx = jnp.take_along_axis(cand_idx, pos, axis=-1)
    g = jax.nn.softmax(top, axis=-1)
    nblk = n // TOKEN_BLOCK

    def experts(args):
        xb, ib, gb = args
        a = jnp.einsum('thkd,td->thk', u_tab[ib], xb)
        w = (jax.nn.gelu(a.astype(jnp.float32)) * gb).astype(xb.dtype)
        return jnp.einsum('thk,thkd->td', w, v_tab[ib])

    out = lax.map(experts, (x.reshape(nblk, TOKEN_BLOCK, D),
                            idx.reshape(nblk, TOKEN_BLOCK, PEER_HEADS, PEER_TOPK),
                            g.reshape(nblk, TOKEN_BLOCK, PEER_HEADS, PEER_TOPK)))
    return out.reshape(B, T, D)

def post_norm_residual(x, y, gate, g, b):
    return layer_norm(DEEPNORM_ALPHA * x + gate * y, g, b)

def trunk_layer(x, mod, lw, rope, ctx_kv):
    (w_in, sg_ln_g, sg_ln_b, w_s, b_s, sink, w_o, ln1_g, ln1_b,
     peer_wq, peer_k1, peer_k2, peer_u, peer_v, ln2_g, ln2_b) = lw
    shift1, scale1, gate1, shift2, scale2, gate2 = mod
    h = x * (1.0 + scale1) + shift1
    q, k, v, su, sv = project_heads(h, w_in)
    sink = sink.reshape(N_KV_HEADS, Q_PER_KV)
    if ctx_kv is None:
        attn = context_attention(q, k, v, sink)
    else:
        q = apply_axial_rope(q, rope)
        k = apply_axial_rope(k, rope)
        attn = latent_attention(q, k, v, ctx_kv[0], ctx_kv[1], sink)
    sg = spatial_gating(su, sv, sg_ln_g, sg_ln_b, w_s, b_s)
    y = jnp.concatenate([attn, sg], axis=-1) @ w_o
    x = post_norm_residual(x, y, gate1, ln1_g, ln1_b)
    h = x * (1.0 + scale2) + shift2
    x = post_norm_residual(x, peer(h, peer_wq, peer_k1, peer_k2, peer_u, peer_v), gate2, ln2_g, ln2_b)
    return x, k, v

def setup_inputs(seed: int = 0) -> dict:
    key = jax.random.key(seed)
    ks = jax.random.split(key, 32)
    f32 = jnp.float32
    nrm = lambda k, shape, s: (jax.random.normal(k, shape, f32) * s)
    D = D_MODEL
    return {
        'x_prompt': nrm(ks[0], (BATCH, SEQ, D), 1.0),
        'x_sample': nrm(ks[1], (DEC_BATCH, DEC_SEQ, D), 1.0),
        'cache_k': nrm(ks[2], (DEC_BATCH, DEPTH, PAST_LEN, N_KV_HEADS, HEAD_DIM), 1.0),
        'cache_v': nrm(ks[3], (DEC_BATCH, DEPTH, PAST_LEN, N_KV_HEADS, HEAD_DIM), 1.0),
        'c': nrm(ks[4], (DEC_BATCH, D), 1.0),
        'c_ctx': nrm(ks[5], (D,), 1.0),
        'w_mod': nrm(ks[6], (DEPTH, D, 6 * D), D ** -0.5),
        'b_mod': nrm(ks[7], (DEPTH, 6 * D), 0.02),
        'w_in': nrm(ks[8], (DEPTH, D, IN_WIDTH), D ** -0.5),
        'sg_ln_g': 1.0 + nrm(ks[9], (DEPTH, SG_WIDTH), 0.02),
        'sg_ln_b': nrm(ks[10], (DEPTH, SG_WIDTH), 0.02),
        'w_s': nrm(ks[11], (DEPTH, SG_GROUPS, SG_CHUNK, SG_CHUNK), SG_CHUNK ** -0.5),
        'b_s': nrm(ks[12], (DEPTH, SG_GROUPS, SG_CHUNK), 0.02),
        'attn_sink': nrm(ks[13], (DEPTH, N_Q_HEADS), 0.1),
        'w_o': nrm(ks[14], (DEPTH, D, D), D ** -0.5 * DEEPNORM_BETA),
        'ln1_g': 1.0 + nrm(ks[15], (DEPTH, D), 0.02),
        'ln1_b': nrm(ks[16], (DEPTH, D), 0.02),
        'peer_wq': nrm(ks[17], (DEPTH, D, PEER_HEADS * PEER_QDIM), D ** -0.5),
        'peer_k1': nrm(ks[18], (DEPTH, PEER_KEYS, PEER_HALF), PEER_HALF ** -0.5),
        'peer_k2': nrm(ks[19], (DEPTH, PEER_KEYS, PEER_HALF), PEER_HALF ** -0.5),
        'peer_u': nrm(ks[20], (DEPTH, PEER_EXPERTS, D), D ** -0.5),
        'peer_v': nrm(ks[21], (DEPTH, PEER_EXPERTS, D), DEEPNORM_BETA),
        'ln2_g': 1.0 + nrm(ks[22], (DEPTH, D), 0.02),
        'ln2_b': nrm(ks[23], (DEPTH, D), 0.02),
    }

def reference(x_prompt, x_sample, cache_k, cache_v, c, c_ctx, w_mod, b_mod, w_in, sg_ln_g, sg_ln_b,
              w_s, b_s, attn_sink, w_o, ln1_g, ln1_b, peer_wq, peer_k1, peer_k2, peer_u, peer_v,
              ln2_g, ln2_b):
    rope = axial_rope(x_sample.shape[1])
    xp = x_prompt
    xs = x_sample
    new_k = []
    new_v = []
    for l in range(DEPTH):
        lw = (w_in[l], sg_ln_g[l], sg_ln_b[l], w_s[l], b_s[l], attn_sink[l], w_o[l], ln1_g[l], ln1_b[l],
              peer_wq[l], peer_k1[l], peer_k2[l], peer_u[l], peer_v[l], ln2_g[l], ln2_b[l])
        mod_ctx = modulation(c_ctx, w_mod[l], b_mod[l])
        mod_lat = modulation(c, w_mod[l], b_mod[l])
        xp, k_l, v_l = trunk_layer(xp, mod_ctx, lw, None, None)
        new_k.append(k_l)
        new_v.append(v_l)
        xs, _, _ = trunk_layer(xs, mod_lat, lw, rope, (cache_k[:, l], cache_v[:, l]))
    state_k = jnp.stack(new_k, axis=1)
    state_v = jnp.stack(new_v, axis=1)
    return (xp, xs, state_k, state_v)


_drawn_inputs = setup_inputs


def setup_inputs(seed=0):
    import zlib

    import numpy as np

    out = dict(_drawn_inputs(seed))
    spreads = {}
    factors = {'sg_ln_g': 4.285, 'sg_ln_b': 4.36, 'b_s': 4.445, 'attn_sink': 55.798}
    for name, (base, spread) in spreads.items():
        noise = np.random.default_rng([zlib.crc32(name.encode()), seed]).standard_normal(out[name].shape)
        drawn = base * np.exp(spread * noise) if base else spread * noise
        out[name] = __import__('jax').numpy.asarray(drawn.astype(out[name].dtype))
    for name, factor in factors.items():
        out[name] = (out[name] * factor).astype(out[name].dtype)
    return out
```

```python
from contextlib import ExitStack

import concourse.bass as bass
from concourse import mybir

F32 = mybir.dt.float32
U32 = mybir.dt.uint32
ALU = mybir.AluOpType
ACT = mybir.ActivationFunctionType
AX = mybir.AxisListType

P = 128
D = 1024
DC = D // P
DEPTH = 2
TILES = 5
GROUPS = {"P": [0], "S": [1, 2, 3, 4]}
HEADS = 8
HD = 64
KV = 2
AW = HEADS * HD
SGG = 8
EXPERTS = 128 * 128
TOPK = 16
PH = 8
SLOTS = PH * TOPK
ALPHA = (2.0 * DEPTH) ** 0.25
EPS = 1e-5
NEG = -8e30
LOWEST = -3.4e38
WR = 5
MR = 6
GR = 8
COLS = 512
IN_COLS = [(0, 512), (512, 256), (768, 512), (1280, 512)]
T_ROWS = 2 * SLOTS
L_ROWS = TILES * T_ROWS
ITERS = SLOTS // GR


def blocks(t):
    return ([t - 1] if t > 0 else []) + [t, 4] + ([t + 1] if t < 3 else [])


def mask_cols(group, t):
    if group == "P":
        return P, 2 * P
    return (0 if t > 0 else P), (4 * P if t < 3 else 3 * P)


def plan_jobs():
    jobs = []
    for g, tiles in GROUPS.items():
        nt = len(tiles)
        jobs += [(("xT", g, c), f"T{c % 2}") for c in range(DC)]
        for n in range(4):
            jobs += [(("in", g, n, t), f"P{t if g == 'S' else n}") for t in range(nt)]
        if g == "S":
            jobs.append((("cT", g), "T1"))
        jobs.append((("kT", g), "T0"))
        for t in range(nt):
            jobs.append((("qT", g, t), "T1"))
            for h in range(HEADS + 1):
                if h < HEADS:
                    jobs.append((("score", g, t, h), "T0"))
                if h:
                    jobs.append((("pT", g, t, h - 1), "T1"))
            jobs.append((("attn", g, t), "O"))
            jobs.append((("gate", g, t), "O"))
            jobs += [(("yT", g, t, half), f"T{half}") for half in range(2)]
        for n in range(2):
            jobs += [(("out", g, n, t), f"P{t if g == 'S' else n}") for t in range(nt)]
        jobs += [(("hT", g, c), f"T{c % 2}") for c in range(DC)]
        for n in range(4):
            for j in range(4):
                jobs.append((("query", g, 4 * n + j), f"P{j}"))
            for j in range(4):
                jobs.append((("keys", g, 4 * n + j), f"T{j % 2}"))
    return jobs


BANK, NTH, TOTAL = {}, {}, {}
for _job, _bank in plan_jobs():
    TOTAL[_bank] = TOTAL.get(_bank, 0) + 1
    BANK[_job], NTH[_job] = _bank, TOTAL[_bank]
MOD_USES = DEPTH * 6


def full_at(job, l):
    return (MOD_USES if BANK[job][0] == "P" else 0) + l * TOTAL[BANK[job]] + NTH[job]


def emptied_at(job, l):
    return full_at(job, l) + 1


def x_at(l, tiles):
    return l * TILES + (tiles + 1)


def build(nc, x_prompt, x_sample, cache_k, cache_v, cond, w_mod, b_col, b_mod, w_in, sg_ln_g, sg_ln_b,
          w_sT, b_sT, attn_sink, w_o, ln1_g, ln1_b, peer_wq, keysT, peer_u, peer_v, ln2_g, ln2_b, consts,
          y_prompt, y_sample, state_k, state_v):
    mod_rows = nc.dram_tensor("mod_rows", (DEPTH, 2, 4, D), F32, kind="Internal").ap()
    tables = (peer_u.rearrange("l e d -> (l e) d"), peer_v.rearrange("l e d -> (l e) d"))

    def chunks(w):
        return w.rearrange("l (c p) n -> l p c n", p=P)

    with ExitStack() as ctx:
        def sb(name, shape, dt=F32):
            return ctx.enter_context(nc.sbuf_tensor(name, shape, dt))

        def sem(name):
            return ctx.enter_context(nc.semaphore(name))

        x = sb("x", [P, TILES, D])
        h2 = sb("h2", [P, TILES, D])
        area = sb("area", [P, 6 * D])
        q_sb = area[:, 0:2048].rearrange("p (t n) -> p t n", t=4)
        su = area[:, 2048:4096].rearrange("p (t n) -> p t n", t=4)
        sv = area[:, 4096:6144].rearrange("p (t n) -> p t n", t=4)
        GATE1, LN1G, LN1B, SCALE2, SHIFT2 = range(5)
        row5 = area[:, 0:5120].rearrange("p (r n) -> p r n", r=5)
        m_slots = area[:, :].rearrange("p (s c n) -> p s c n", s=MR, c=2)
        row3 = sb("row3", [P, 3, D])
        sg_rows = sb("sg_rows", [P, 2, AW])
        ring = sb("ring", [P, GR, D])
        w_ring = sb("w_ring", [P, WR, 2, COLS])
        hT = sb("hT", [P, DC, 512])
        qT = sb("qT", [P, 4, P])
        k_sb = sb("k_sb", [P, 5, P])
        v_sb = sb("v_sb", [P, 5, P])
        kT = sb("kT", [P, 5, P])
        probs = sb("probs", [P, 2, 512])
        pT = sb("pT", [P, 2, 512])
        mask = sb("mask", [P, 512])
        cst = sb("cst", [P, 2 * 4 * HD + TOPK])
        rope = cst[:, 0:2 * 4 * HD].rearrange("p (a t n) -> p a t n", a=2, t=4)
        iota = cst[:, 2 * 4 * HD:]
        wsT = sb("wsT", [P, SGG, P])
        bsT = sb("bsT", [P, SGG])
        sink = sb("sink", [P, HEADS])
        keys = sb("keys", [P, 2, P])
        best = sb("best", [P, 4, 2 * PH, TOPK])
        best_ix = sb("best_ix", [P, 4, 2 * PH, TOPK], U32)
        ixf = sb("ixf", [P, 2 * PH, TOPK])
        left = sb("left", [P, P])
        cand = sb("cand", [P, 4, 256])
        onehot = sb("onehot", [P, 4, TOPK, TOPK])
        top = sb("top", [P, PH, TOPK])
        pos = sb("pos", [P, PH, TOPK], U32)
        part = sb("part", [P, PH, TOPK], U32)
        hi = sb("hi", [P, PH, TOPK])
        lo = sb("lo", [P, PH, TOPK])
        r1 = sb("r1", [P, PH, TOPK])
        r2 = sb("r2", [P, PH, TOPK])
        eidx = sb("eidx", [P, 2, SLOTS], U32)
        idx_stage = sb("idx_stage", [P, 2 * GR], U32)
        gsm = sb("gsm", [P, 2, PH, TOPK])
        gsum = sb("gsum", [P, PH])
        dots = sb("dots", [P, SLOTS])
        gel = sb("gel", [P, SLOTS])
        wexp = sb("wexp", [P, SLOTS])
        tmp = sb("tmp", [P, 512])
        acc = sb("acc", [P, D])
        qh = probs
        ident = sb("ident", [P, P])
        cT = sb("cT", [P, DC, 2])
        bcol = sb("bcol", [P, DEPTH, 16])
        mcol = sb("mcol", [P, DEPTH, 16, 2])
        stats = sb("stats", [P, 2, 6])
        mv = sb("mv", [P, 2])
        rstd = sb("rstd", [P, 1])
        nr = sb("nr", [P, 3])
        guess = sb("guess", [P, 1], U32)
        negmax = sb("negmax", [P, 2, HEADS])
        maxs = sb("maxs", [P, 2, HEADS])
        rsum = sb("rsum", [P, 2, HEADS])
        esink = sb("esink", [P, HEADS])
        den = sb("den", [P, HEADS])
        layer_base = sb("layer_base", [P, 1])

        bank = {b: ctx.enter_context(nc.psum_tensor(b, [P, 512], F32))
                for b in ("P0", "P1", "P2", "P3", "T0", "T1", "O")}

        full = {b: sem(f"full_{b}") for b in bank}
        emptied = {b: sem(f"emptied_{b}") for b in bank}
        const_in = sem("const_in")
        built = sem("built")
        silu_done = sem("silu_done")
        bcol_done = sem("bcol_done")
        m_full = [sem(f"m_full{i}") for i in range(MR)]
        m_used = sem("m_used")
        brow_in = sem("brow_in")
        mod_stored = sem("mod_stored")
        w_full = [sem(f"w_full{i}") for i in range(WR)]
        w_used = sem("w_used")
        layer_in = sem("layer_in")
        rows_in = sem("rows_in")
        gate2_in = sem("gate2_in")
        state_out = sem("state_out")
        sv_ready = sem("sv_ready")
        probs_max = sem("probs_max")
        probs_done = sem("probs_done")
        sink_in = sem("sink_in")
        sink_exp = sem("sink_exp")
        h2_ready = sem("h2_ready")
        top_ready = sem("top_ready")
        top_exp = sem("top_exp")
        idx_ready = sem("idx_ready")
        staged = sem("staged")
        row_full = [sem(f"row_full{i}") for i in range(GR)]
        row_used = sem("row_used")
        gelu_done = sem("gelu_done")
        x_done = sem("x_done")
        vchain = sem("vchain")
        y_out = sem("y_out")
        passed = sem("passed")

        def held(eng):
            eng.sem_inc(passed, 1)

        block = ctx.enter_context(nc.Block())

        @block.sync
        def _(sp):
            sp.dma_start(cT[:], cond).then_inc(const_in, 16)
            sp.dma_start(bcol[:], b_col).then_inc(const_in, 16)
            sp.dma_start(cst[:], consts).then_inc(const_in, 16)
            sp.dma_start(x[:, 0, :], x_prompt[0]).then_inc(const_in, 16)
            sp.dma_start(x[:, 1:5, :], x_sample[0].rearrange("(t p) d -> p t d", p=P)).then_inc(const_in, 16)
            with sp.Fori(0, DEPTH) as l:
                sp.wait_ge(emptied["P3"], l * 6 + 1)
                sp.dma_start(h2[0:2, 0:4, :], b_mod[l, 2 * D:6 * D].rearrange("(a r n) -> a r n", a=1, n=D)
                             .rearrange("a r n -> (a r) n").partition_broadcast(2)).then_inc(brow_in, 16)
                for n in range(12):
                    for q in range(4):
                        u = 4 * n + q
                        if u >= MR:
                            pn, pq = divmod(u - MR, 4)
                            if pq < 3:
                                sp.wait_ge(m_used, l * 36 + 3 * pn + pq + 1)
                            else:
                                sp.wait_ge(full["P3" if pn < 4 else f"P{pn % 4}"],
                                           l * 6 + (pn + 1 if pn < 4 else 4 + pn // 4))
                        sp.dma_start(m_slots[:, u % MR], chunks(w_mod)[l, :, 2 * q:2 * q + 2, n * COLS:(n + 1) * COLS]
                                     ).then_inc(m_full[u % MR], 16)
                for b in range(4):
                    sp.wait_ge(emptied[f"P{b}"], (l + 1) * 6 + 1)
                sp.dma_start(mod_rows[l].rearrange("a r n -> a (r n)"),
                             hT[0:2, :, :].rearrange("a c n -> a (c n)")).then_inc(mod_stored, 16)
                sp.wait_ge(mod_stored, (l + 1) * 16)
                held(sp)
            with sp.Fori(0, DEPTH) as l:
                sp.wait_ge(x_done, x_at(l, 0))
                sp.dma_start(wsT[:], w_sT[l]).then_inc(layer_in, 16)
                sp.dma_start(bsT[:], b_sT[l]).then_inc(layer_in, 16)
                sp.dma_start(keys[:], keysT[l]).then_inc(layer_in, 16)
                sp.dma_start(sink[:], attn_sink[l].partition_broadcast(P)).then_inc(layer_in, 16)
                sp.dma_start(sg_rows[:, 0, :], sg_ln_g[l].partition_broadcast(P)).then_inc(layer_in, 16)
                sp.dma_start(sg_rows[:, 1, :], sg_ln_b[l].partition_broadcast(P)).then_inc(layer_in, 16)
                sp.dma_start(k_sb[:, 4, :], cache_k[0, l].rearrange("s a d -> s (a d)")).then_inc(layer_in, 16)
                sp.dma_start(v_sb[:, 4, :], cache_v[0, l].rearrange("s a d -> s (a d)")).then_inc(layer_in, 16)
                sp.dma_start(row3[:, 0, :], mod_rows[l, 0, 3].partition_broadcast(P)).then_inc(layer_in, 16)
                sp.dma_start(row3[:, 1, :], ln2_g[l].partition_broadcast(P)).then_inc(layer_in, 16)
                sp.dma_start(row3[:, 2, :], ln2_b[l].partition_broadcast(P)).then_inc(layer_in, 16)
                use = 0
                ends = []
                wu = 0
                for gi, g in enumerate(GROUPS):
                    last = len(GROUPS[g]) - 1
                    plan = [("in", n, w_in, c0, w) for n, (c0, w) in enumerate(IN_COLS)]
                    plan += [("out", n, w_o, n * COLS, COLS) for n in range(2)]
                    plan += [("query", n, peer_wq, n * COLS, COLS) for n in range(4)]
                    for kind, n, w, c0, width in plan:
                        if kind == "query" and n == 0:
                            sp.wait_ge(full["T1"], full_at(("yT", g, last, 1), l))
                            held(sp)
                            for r, src in ((GATE1, mod_rows[l, gi, 0]), (LN1G, ln1_g[l]), (LN1B, ln1_b[l]),
                                           (SCALE2, mod_rows[l, gi, 2]), (SHIFT2, mod_rows[l, gi, 1])):
                                sp.dma_start(row5[:, r, :], src.partition_broadcast(P)).then_inc(rows_in, 16)
                        for q in range(4):
                            if use >= WR:
                                s, v = ends[use - WR]
                                sp.wait_ge(s, l * 60 + v if s is w_used else full_at(v, l))
                            sp.dma_start(w_ring[:, use % WR, :, 0:width],
                                         chunks(w)[l, :, 2 * q:2 * q + 2, c0:c0 + width]
                                         ).then_inc(w_full[use % WR], 16)
                            if q < 3:
                                wu += 1
                                ends.append((w_used, wu))
                            else:
                                job = (kind, g, 4 * n + 3) if kind == "query" else (kind, g, n, last)
                                ends.append((full[BANK[job]], job))
                            use += 1
                    if g == "P":
                        sp.wait_ge(emptied[BANK["in", "P", 1, 0]], emptied_at(("in", "P", 1, 0), l))
                        sp.dma_start(state_k[0, l].rearrange("s a d -> s (a d)"), k_sb[:, 0, :]).then_inc(state_out, 16)
                        sp.dma_start(state_v[0, l].rearrange("s a d -> s (a d)"), v_sb[:, 0, :]).then_inc(state_out, 16)
            sp.wait_ge(x_done, x_at(DEPTH, 0))
            sp.dma_start(y_prompt[0], x[:, 0, :]).then_inc(y_out, 16)
            sp.dma_start(y_sample[0].rearrange("(t p) d -> p t d", p=P), x[:, 1:5, :]).then_inc(y_out, 16)
            sp.wait_ge(y_out, 32)
            sp.wait_ge(state_out, 32 * DEPTH)

        @block.gpsimd
        def _(pool):
            pool.memset(ident[:], 0.0).then_inc(built, 1)
            pool.memset(mask[:], 0.0).then_inc(built, 1)
            pool.wait_ge(built, 2)
            pool.affine_select(out=ident[:], in_=ident[:], compare_op=ALU.not_equal, fill=1.0, base=0,
                               pattern=[[-1, P]], channel_multiplier=1).then_inc(built, 1)
            pool.affine_select(out=mask[:, 0:P], in_=mask[:, 0:P], compare_op=ALU.is_ge, fill=NEG, base=0,
                               pattern=[[1, P]], channel_multiplier=-1).then_inc(built, 1)
            pool.affine_select(out=mask[:, 3 * P:4 * P], in_=mask[:, 3 * P:4 * P], compare_op=ALU.is_ge, fill=NEG,
                               base=0, pattern=[[-1, P]], channel_multiplier=1).then_inc(built, 1)

            def fetch(l, k, phase, i, first):
                for s in range(2):
                    row = l * L_ROWS + i * 2 * GR + (k * T_ROWS + phase * SLOTS + s * GR)
                    if not (first and s == 0):
                        pool.wait_ge(row_used, row - (GR - 1))
                        held(pool)
                    src = i * 2 * GR + s * GR
                    pool.tensor_copy(idx_stage[:, s * GR:(s + 1) * GR],
                                     eidx[:, k % 2, bass.ds(src, GR)]).then_inc(staged, 1)
                    pool.wait_ge(staged, l * (L_ROWS // GR) + i * 2 + ((k * T_ROWS + phase * SLOTS) // GR + s + 1))
                    held(pool)
                    for b in range(GR):
                        if b and not (first and s == 0):
                            pool.wait_ge(row_used, row + (b - GR + 1))
                            held(pool)
                        pool.indirect_dma_start(
                            out=ring[:, b, :], out_offset=None, in_=tables[phase],
                            in_offset=bass.IndirectOffsetOnAxis(ap=idx_stage[:, s * GR + b:s * GR + b + 1], axis=0),
                        ).then_inc(row_full[b], 16)

            with pool.Fori(0, DEPTH) as l:
                for k in range(TILES):
                    pool.wait_ge(idx_ready, l * TILES + (k + 1))
                    held(pool)
                    for phase in range(2):
                        first = k == 0 and phase == 0
                        if first:
                            fetch(l, k, phase, 0, True)
                        with pool.Fori(int(first), ITERS // 2) as i:
                            fetch(l, k, phase, i, False)
                        if k == 1 and phase == 0:
                            pool.wait_ge(x_done, x_at(l, 1))
                            pool.dma_start(row3[:, 0, :], mod_rows[l, 1, 3].partition_broadcast(P)
                                           ).then_inc(gate2_in, 16)

        @block.tensor
        def _(pe):
            pe.wait_ge(silu_done, 1)
            with pe.Fori(0, DEPTH) as l:
                for n in range(12):
                    for q in range(4):
                        u = 4 * n + q
                        pe.wait_ge(m_full[u % MR], l * (16 * 48 // MR) + 16 * (u // MR + 1))
                        for j in range(4 if n < 4 else 1):
                            b = f"P{j if n < 4 else n % 4}"
                            if q == 0:
                                pe.wait_ge(emptied[b], l * 6 + (n + 1 if n < 4 else 4 + n // 4))
                            for c in (2 * q, 2 * q + 1):
                                if n < 4:
                                    mm = pe.matmul(bank[b][:, 0:2], m_slots[:, u % MR, c % 2, j * P:(j + 1) * P],
                                                   cT[:, c, :], start=c == 0, stop=c == DC - 1)
                                else:
                                    mm = pe.matmul(bank[b][0:2, :], cT[:, c, :], m_slots[:, u % MR, c % 2, :],
                                                   start=c == 0, stop=c == DC - 1)
                            if q == 3:
                                mm.then_inc(full[b], 1)
                        if q < 3:
                            mm.then_inc(m_used, 1)

            pe.wait_ge(built, 5)
            pe.wait_ge(mod_stored, 16 * DEPTH)
            with pe.Fori(0, DEPTH) as l:
                use = [0]

                def begin(job):
                    pe.wait_ge(emptied[BANK[job]], emptied_at(job, l) - 1)
                    return bank[BANK[job]]

                def finish(mm, job):
                    mm.then_inc(full[BANK[job]], 1)

                def taken(job):
                    pe.wait_ge(emptied[BANK[job]], emptied_at(job, l))

                def slot():
                    s = use[0] % WR
                    pe.wait_ge(w_full[s], l * (80 // WR * 16) + 16 * (use[0] // WR + 1))
                    use[0] += 1
                    return w_ring[:, s]

                def project(kind, g, n, width):
                    nt = len(GROUPS[g])
                    for q in range(4):
                        w = slot()
                        for t in range(nt):
                            job = (kind, g, n, t)
                            out = begin(job) if q == 0 else bank[BANK[job]]
                            for c in (2 * q, 2 * q + 1):
                                mm = pe.matmul(out[:, 0:width], hT[:, c, t * P:(t + 1) * P], w[:, c % 2, 0:width],
                                               start=c == 0, stop=c == DC - 1)
                            if q == 3:
                                finish(mm, job)
                        if q < 3:
                            mm.then_inc(w_used, 1)

                def attend(g, t):
                    job = ("qT", g, t)
                    out = begin(job)
                    for pair in range(4):
                        mm = pe.transpose(out[:, pair * P:(pair + 1) * P], q_sb[:, t, pair * P:(pair + 1) * P], ident[:])
                    finish(mm, job)
                    taken(job)
                    keyb = blocks(t) if g == "S" else [0]
                    ao = begin(("attn", g, t))
                    heads = (GROUPS[g][0] + t) * HEADS
                    for h in range(HEADS + 1):
                        if h < HEADS:
                            job = ("score", g, t, h)
                            out = begin(job)
                            a = HD * (h // 4)
                            for i, kb in enumerate(keyb):
                                mm = pe.matmul(out[:, i * P:(i + 1) * P], qT[a:a + HD, h % 4, :], kT[a:a + HD, kb, :],
                                               start=True, stop=True)
                            finish(mm, job)
                        if h:
                            hh = h - 1
                            job = ("pT", g, t, hh)
                            out = begin(job)
                            pe.wait_ge(probs_done, l * (TILES * HEADS) + (heads + hh + 1))
                            for i in range(len(keyb)):
                                mm = pe.transpose(out[:, i * P:(i + 1) * P], probs[:, hh % 2, i * P:(i + 1) * P], ident[:])
                            finish(mm, job)
                            taken(job)
                            a = HD * (hh // 4)
                            for i, kb in enumerate(keyb):
                                mm = pe.matmul(ao[:, hh * HD:(hh + 1) * HD], pT[:, hh % 2, i * P:(i + 1) * P],
                                               v_sb[:, kb, a:a + HD], start=i == 0, stop=i == len(keyb) - 1)
                    finish(mm, ("attn", g, t))

                for g, tiles in GROUPS.items():
                    nt = len(tiles)
                    if g == "P":
                        pe.wait_ge(x_done, x_at(l, 0))
                        pe.wait_ge(const_in, 16 * 5)
                    for c in range(DC):
                        job = ("xT", g, c)
                        out = begin(job)
                        for t, k in enumerate(tiles):
                            mm = pe.transpose(out[:, t * P:(t + 1) * P], x[:, k, c * P:(c + 1) * P], ident[:])
                        finish(mm, job)
                    taken(("xT", g, DC - 2))
                    taken(("xT", g, DC - 1))
                    for n, (_, width) in enumerate(IN_COLS):
                        project("in", g, n, width)
                    pe.wait_ge(layer_in, (l + 1) * (16 * 11))
                    if g == "S":
                        job = ("cT", g)
                        finish(pe.transpose(begin(job)[:, 0:P], k_sb[:, 4, :], ident[:]), job)
                        taken(job)
                    job = ("kT", g)
                    out = begin(job)
                    for t in range(nt):
                        taken(("in", g, 1, t))
                        mm = pe.transpose(out[:, t * P:(t + 1) * P], k_sb[:, t, :], ident[:])
                    finish(mm, job)
                    taken(job)
                    for t in range(nt):
                        attend(g, t)
                        job = ("gate", g, t)
                        out = begin(job)
                        pe.wait_ge(sv_ready, l * TILES + (tiles[t] + 1))
                        for s in range(SGG):
                            mm = pe.matmul(out[:, s * HD:(s + 1) * HD], wsT[:, s, :], sv[:, t, s * HD:(s + 1) * HD],
                                           start=True, stop=True)
                        finish(mm, job)
                        taken(job)
                        for half, src in ((0, q_sb), (1, su)):
                            job = ("yT", g, t, half)
                            out = begin(job)
                            for c in range(4):
                                mm = pe.transpose(out[:, c * P:(c + 1) * P], src[:, t, c * P:(c + 1) * P], ident[:])
                            finish(mm, job)
                    taken(("yT", g, nt - 1, 0))
                    taken(("yT", g, nt - 1, 1))
                    for n in range(2):
                        project("out", g, n, COLS)
                    pe.wait_ge(h2_ready, l * TILES + (tiles[-1] + 1))
                    for c in range(DC):
                        job = ("hT", g, c)
                        out = begin(job)
                        for t, k in enumerate(tiles):
                            mm = pe.transpose(out[:, t * P:(t + 1) * P], h2[:, k, c * P:(c + 1) * P], ident[:])
                        finish(mm, job)
                    taken(("hT", g, DC - 2))
                    taken(("hT", g, DC - 1))
                    for n in range(4):
                        for q in range(4):
                            w = slot()
                            for j in range(4):
                                job = ("query", g, 4 * n + j)
                                out = begin(job) if q == 0 else bank[BANK[job]]
                                for c in (2 * q, 2 * q + 1):
                                    mm = pe.matmul(out[:, 0:nt * P], w[:, c % 2, j * P:(j + 1) * P], hT[:, c, 0:nt * P],
                                                   start=c == 0, stop=c == DC - 1)
                                if q == 3:
                                    finish(mm, job)
                            if q < 3:
                                mm.then_inc(w_used, 1)
                        for j in range(4):
                            job = ("keys", g, 4 * n + j)
                            out = begin(job)
                            taken(("query", g, 4 * n + j))
                            for t in range(nt):
                                mm = pe.matmul(out[:, t * P:(t + 1) * P], qh[:, j % 2, t * P:(t + 1) * P],
                                               keys[:, j % 2, :], start=True, stop=True)
                            finish(mm, job)

        @block.scalar
        def _(act):
            act.wait_ge(const_in, 16 * 5)
            act.activation(cT[:], cT[:], ACT.Silu).then_inc(silu_done, 1)
            act.wait_ge(bcol_done, 1)
            with act.Fori(0, DEPTH) as l:
                for n in range(4):
                    for j in range(4):
                        act.wait_ge(full[f"P{j}"], l * 6 + (n + 1))
                        act.activation(mcol[:, bass.ds(l, 1), 4 * n + j, :].rearrange("p a c -> p (a c)"),
                                       bank[f"P{j}"][:, 0:2], ACT.Identity,
                                       bias=bcol[:, bass.ds(l, 1), 4 * n + j]
                                       ).then_inc(emptied[f"P{j}"], 1)

            with act.Fori(0, DEPTH) as l:
                def ready(job):
                    act.wait_ge(full[BANK[job]], full_at(job, l))
                    return bank[BANK[job]]

                def attend(g, t):
                    k = GROUPS[g][t]
                    job = ("qT", g, t)
                    act.activation(qT[:].rearrange("p a n -> p (a n)"), ready(job)[:, :], ACT.Copy
                                   ).then_inc(emptied[BANK[job]], 1)
                    lo_col, hi_col = mask_cols(g, t)
                    width = hi_col - lo_col
                    for h in range(HEADS + 1):
                        if h < HEADS:
                            n = k * HEADS + h
                            act.wait_ge(probs_max, l * (TILES * HEADS) + (n + 1))
                            act.activation(probs[:, h % 2, 0:width], probs[:, h % 2, 0:width], ACT.Exp,
                                           bias=negmax[:, k % 2, h:h + 1], accum_out=rsum[:, k % 2, h:h + 1]
                                           ).then_inc(probs_done, 1)
                        if h:
                            job = ("pT", g, t, h - 1)
                            act.activation(pT[:, (h - 1) % 2, 0:width], ready(job)[:, 0:width], ACT.Copy
                                           ).then_inc(emptied[BANK[job]], 1)
                    act.wait_ge(sink_in, l * TILES + (k + 1))
                    act.activation(esink[:], esink[:], ACT.Exp).then_inc(sink_exp, 1)

                def top_softmax(k):
                    act.wait_ge(top_ready, l * TILES + (k + 1))
                    act.activation(gsm[:, k % 2], gsm[:, k % 2], ACT.Exp).then_inc(top_exp, 1)

                def gelu_dots(k):
                    act.wait_ge(row_used, l * L_ROWS + (k * T_ROWS + SLOTS))
                    act.activation(gel[:], dots[:], ACT.Gelu_apprx_tanh).then_inc(gelu_done, 1)

                for gi, (g, tiles) in enumerate(GROUPS.items()):
                    nt = len(tiles)
                    for c in range(DC):
                        job = ("xT", g, c)
                        act.activation(hT[:, c, 0:nt * P], ready(job)[:, 0:nt * P], ACT.Identity,
                                       scale=mcol[:, bass.ds(l, 1), 8 + c, gi],
                                       bias=mcol[:, bass.ds(l, 1), c, gi]).then_inc(emptied[BANK[job]], 1)
                    for n, dst in ((2, su), (3, sv)):
                        for t in range(nt):
                            job = ("in", g, n, t)
                            act.activation(dst[:, t, :], ready(job)[:, :], ACT.Gelu_apprx_tanh
                                           ).then_inc(emptied[BANK[job]], 1)
                    if g == "S":
                        job = ("cT", g)
                        act.activation(kT[:, 4, :], ready(job)[:, 0:P], ACT.Copy).then_inc(emptied[BANK[job]], 1)
                    job = ("kT", g)
                    act.activation(kT[:, 0:nt, :].rearrange("p t n -> p (t n)"), ready(job)[:, 0:nt * P], ACT.Copy
                                   ).then_inc(emptied[BANK[job]], 1)
                    for t in range(nt):
                        attend(g, t)
                        for half in range(2):
                            job = ("yT", g, t, half)
                            act.activation(hT[:, 4 * half:4 * half + 4, t * P:(t + 1) * P],
                                           ready(job)[:, :].rearrange("p (c n) -> p c n", c=4), ACT.Copy
                                           ).then_inc(emptied[BANK[job]], 1)
                    if g == "S":
                        gelu_dots(0)
                    for c in range(DC):
                        job = ("hT", g, c)
                        act.activation(hT[:, c, 0:nt * P], ready(job)[:, 0:nt * P], ACT.Copy
                                       ).then_inc(emptied[BANK[job]], 1)
                    for j in range(2 * PH):
                        job = ("query", g, j)
                        src = ready(job)
                        if j >= 2:
                            ready(("keys", g, j - 2))
                        act.activation(qh[:, j % 2, 0:nt * P], src[:, 0:nt * P], ACT.Copy
                                       ).then_inc(emptied[BANK[job]], 1)
                    top_softmax(tiles[0])
                for k in range(1, TILES):
                    if k + 1 < TILES:
                        top_softmax(k + 1)
                    gelu_dots(k)

        @block.vector
        def _(dve):
            for b in bank:
                dve.sem_inc(emptied[b], 1)
            dve.sem_inc(x_done, 1)
            dve.memset(layer_base[:], 0.0).then_inc(vchain, 1)
            dve.wait_ge(vchain, 1)
            dve.sem_clear(vchain)
            dve.wait_ge(const_in, 16 * 5)
            dve.tensor_scalar(bcol[:, :, 8:16], bcol[:, :, 8:16], 1.0, None, ALU.add).then_inc(bcol_done, 1)
            with dve.Fori(0, DEPTH) as l:
                dve.wait_ge(brow_in, (l + 1) * 16)
                for n in range(4, 12):
                    b = f"P{n % 4}"
                    dve.wait_ge(full[b], l * 6 + (4 + n // 4))
                    row, col = divmod((n - 4) * COLS, D)
                    dve.scalar_tensor_tensor(hT[0:2, n - 4, :], bank[b][0:2, :], 1.0 if row == 2 else 0.0,
                                             h2[0:2, row, col:col + COLS], ALU.add, ALU.add
                                             ).then_inc(emptied[b], 1)

            with dve.Fori(0, DEPTH) as l:
                chain = [0]

                def link(ins):
                    chain[0] += 1
                    ins.then_inc(vchain, 1)
                    dve.wait_ge(vchain, chain[0])

                def ready(job):
                    dve.wait_ge(full[BANK[job]], full_at(job, l))
                    return bank[BANK[job]]

                def empty(ins, job):
                    ins.then_inc(emptied[BANK[job]], 1)
                    dve.wait_ge(emptied[BANK[job]], emptied_at(job, l))

                def layer_norm_stats(src, width):
                    n = width // 512
                    for i in range(n):
                        link(dve.bn_stats(stats[:, i, :], src[:, i * 512:(i + 1) * 512]))
                    link(dve.bn_aggr(mv[:], stats[:, 0:n, :]))
                    link(dve.tensor_scalar(nr[:, 0:1], mv[:, 1:2], EPS, None, ALU.add))
                    link(dve.tensor_scalar(nr[:, 1:2], nr[:, 0:1], -0.5, None, ALU.mult))
                    link(dve.tensor_single_scalar(guess[:], nr[:, 0:1].bitcast(U32), 1, ALU.logical_shift_right))
                    link(dve.tensor_scalar(rstd[:].bitcast(U32), guess[:], -1.0, float(0x5f3759df), ALU.mult, ALU.add))
                    for _ in range(3):
                        link(dve.scalar_tensor_tensor(nr[:, 2:3], rstd[:], nr[:, 1:2], rstd[:], ALU.mult, ALU.mult))
                        link(dve.scalar_tensor_tensor(rstd[:], nr[:, 2:3], 1.5, rstd[:], ALU.add, ALU.mult))
                    link(dve.tensor_scalar(src, src, mv[:, 0:1], rstd[:, 0:1], ALU.subtract, ALU.mult))

                def dot_rows(k, i0, i1):
                    held(dve)
                    with dve.Fori(i0, i1) as i:
                        for b in range(GR):
                            dve.wait_ge(row_full[b], l * (16 * L_ROWS // GR) + i * 16 + 16 * (k * 2 * ITERS + 1))
                            dve.scalar_tensor_tensor(ring[:, b, :], ring[:, b, :], 1.0, h2[:, k, :], ALU.mult, ALU.mult,
                                                     accum_out=dots[:, bass.ds(i * GR + b, 1)]).then_inc(row_used, 1)

                def expert_weights(k):
                    dve.wait_ge(gelu_done, l * TILES + (k + 1))
                    link(dve.tensor_tensor(wexp[:], gel[:], gsm[:, k % 2].rearrange("p h j -> p (h j)"), ALU.mult))
                    link(dve.memset(acc[:], 0.0))

                def add_rows(k, i0, i1):
                    held(dve)
                    with dve.Fori(i0, i1) as i:
                        for b in range(GR):
                            dve.wait_ge(row_full[b], l * (16 * L_ROWS // GR) + i * 16
                                        + 16 * (k * 2 * ITERS + ITERS + 1))
                            dve.wait_ge(row_used, l * L_ROWS + i * GR + (k * T_ROWS + SLOTS + b))
                            dve.scalar_tensor_tensor(acc[:], ring[:, b, :], wexp[:, bass.ds(i * GR + b, 1)], acc[:],
                                                     ALU.mult, ALU.add).then_inc(row_used, 1)

                def finish_tile(k):
                    dve.wait_ge(row_used, l * L_ROWS + (k + 1) * T_ROWS)
                    if k == 1:
                        dve.wait_ge(gate2_in, (l + 1) * 16)
                    link(dve.tensor_tensor(acc[:], acc[:], row3[:, 0, :], ALU.mult))
                    link(dve.scalar_tensor_tensor(x[:, k, :], x[:, k, :], ALPHA, acc[:], ALU.mult, ALU.add))
                    layer_norm_stats(x[:, k, :], D)
                    link(dve.tensor_tensor(x[:, k, :], x[:, k, :], row3[:, 1, :], ALU.mult))
                    dve.tensor_tensor(x[:, k, :], x[:, k, :], row3[:, 2, :], ALU.add).then_inc(x_done, 1)
                    dve.wait_ge(x_done, x_at(l, k + 1))

                unit = [0]

                def prompt_rows(n):
                    if unit[0] < ITERS:
                        assert unit[0] + n <= ITERS
                        dot_rows(0, unit[0], unit[0] + n)
                    else:
                        if unit[0] == ITERS:
                            expert_weights(0)
                        add_rows(0, unit[0] - ITERS, unit[0] - ITERS + n)
                    unit[0] += n
                    if unit[0] == 2 * ITERS:
                        finish_tile(0)

                def half_keys(g, j):
                    job = ("keys", g, j)
                    out = ready(job)
                    held(dve)
                    nt = len(GROUPS[g])
                    for t in range(nt):
                        s = out[:, t * P:(t + 1) * P]
                        link(dve.max(best[:, t, j, 0:8], s))
                        link(dve.max_index(best_ix[:, t, j, 0:8], best[:, t, j, 0:8], s))
                        ins = dve.match_replace(left[:], best[:, t, j, 0:8], s, LOWEST)
                        if t == nt - 1:
                            empty(ins, job)
                        else:
                            link(ins)
                        if t == nt - 1:
                            held(dve)
                        link(dve.max(best[:, t, j, 8:16], left[:]))
                        link(dve.max_index(best_ix[:, t, j, 8:16], best[:, t, j, 8:16], left[:]))

                def best_pairs(t, half):
                    pair = best[:, t].rearrange("p (h a) j -> p h a j", a=2)[:, 4 * half:4 * half + 4]
                    link(dve.tensor_tensor(cand[:].rearrange("p h (i j) -> p h i j", i=TOPK),
                                           pair[:, :, 0, :].unsqueeze(3).to_broadcast([P, 4, TOPK, TOPK]),
                                           pair[:, :, 1, :].unsqueeze(2).to_broadcast([P, 4, TOPK, TOPK]), ALU.add))
                    for i in range(4):
                        h = 4 * half + i
                        link(dve.max(top[:, h, 0:8], cand[:, i, :]))
                        link(dve.max_index(pos[:, h, 0:8], top[:, h, 0:8], cand[:, i, :]))
                        link(dve.match_replace(cand[:, i, :], top[:, h, 0:8], cand[:, i, :], LOWEST))
                        link(dve.max(top[:, h, 8:16], cand[:, i, :]))
                        link(dve.max_index(pos[:, h, 8:16], top[:, h, 8:16], cand[:, i, :]))

                def softmax_in(k):
                    dve.tensor_tensor(gsm[:, k % 2], top[:], top[:, :, 0:1].to_broadcast([P, PH, TOPK]),
                                      ALU.subtract).then_inc(top_ready, 1)

                def split_positions(t):
                    link(dve.tensor_copy(ixf[:], best_ix[:, t]))
                    link(dve.tensor_single_scalar(part[:], pos[:], 4, ALU.logical_shift_right))
                    link(dve.tensor_copy(hi[:], part[:]))
                    link(dve.tensor_single_scalar(part[:], pos[:], 15, ALU.bitwise_and))
                    link(dve.tensor_copy(lo[:], part[:]))

                def pick(half, which):
                    src, dst = ((hi, r1), (lo, r2))[which]
                    hs = slice(4 * half, 4 * half + 4)
                    shape = [P, 4, TOPK, TOPK]
                    num = ixf[:].rearrange("p (h a) j -> p h a j", a=2)[:, hs, which, :]
                    link(dve.tensor_tensor(onehot[:], src[:, hs, :].unsqueeze(3).to_broadcast(shape),
                                           iota.unsqueeze(1).unsqueeze(1).to_broadcast(shape), ALU.is_equal))
                    link(dve.tensor_tensor(onehot[:], onehot[:], num.unsqueeze(2).to_broadcast(shape), ALU.mult))
                    link(dve.tensor_reduce(dst[:, hs, :], onehot[:], AX.X, ALU.add))

                def expert_numbers(k):
                    link(dve.scalar_tensor_tensor(r1[:], r1[:], 128.0, r2[:], ALU.mult, ALU.add))
                    dve.tensor_scalar(eidx[:, k % 2, :].rearrange("p (h j) -> p h j", h=PH), r1[:],
                                      layer_base[:, 0:1], None, ALU.add).then_inc(idx_ready, 1)
                    dve.wait_ge(top_exp, l * TILES + (k + 1))
                    link(dve.tensor_reduce(gsum[:], gsm[:, k % 2], AX.X, ALU.add))
                    link(dve.reciprocal(gsum[:], gsum[:]))
                    link(dve.tensor_tensor(gsm[:, k % 2], gsm[:, k % 2],
                                           gsum[:].unsqueeze(2).to_broadcast([P, PH, TOPK]), ALU.mult))
                    dve.wait_ge(idx_ready, l * TILES + (k + 1))

                def choose(k, t, step):
                    if step == 0:
                        best_pairs(t, 0)
                    elif step == 1:
                        best_pairs(t, 1)
                        softmax_in(k)
                    elif step == 2:
                        split_positions(t)
                        pick(0, 0)
                        pick(0, 1)
                    else:
                        pick(1, 0)
                        pick(1, 1)
                        expert_numbers(k)

                def rotate(src, dst, t, nh, perm):
                    n = nh * HD
                    c, s = rope[:, 0, t, :], rope[:, 1, t, :]
                    if perm:
                        v = src.rearrange("p (a b d) -> p a b d", a=2, d=HD)
                        shape = [P, 2, 4, HD]
                        o = dst.rearrange("p (b a d) -> p a b d", a=2, d=HD)
                        cb = c.unsqueeze(1).unsqueeze(1).to_broadcast(shape)
                        swapped = tmp[:, 0:n].rearrange("p (a b d) -> p a b d", a=2, d=HD)
                    else:
                        v = src.rearrange("p (a d) -> p a d", d=HD)
                        shape = [P, nh, HD]
                        o = dst.rearrange("p (a d) -> p a d", d=HD)
                        cb = c.unsqueeze(1).to_broadcast(shape)
                        swapped = tmp[:, 0:n].rearrange("p (a d) -> p a d", d=HD)
                    link(dve.tensor_tensor(o, v, cb, ALU.mult))
                    x4 = src.rearrange("p (a e f) -> p a e f", e=4, f=16)
                    y4 = tmp[:, 0:n].rearrange("p (a e f) -> p a e f", e=4, f=16)
                    s4 = s.rearrange("p (e f) -> p e f", e=4)
                    for z in range(2):
                        link(dve.tensor_tensor(y4[:, :, z::2, :], x4[:, :, 1 - z::2, :],
                                               s4[:, z::2, :].unsqueeze(1).to_broadcast([P, nh, 2, 16]), ALU.mult))
                    return dve.tensor_tensor(o, o, swapped, ALU.add)

                def take_qk(g, n, t):
                    job = ("in", g, n, t)
                    out = ready(job)
                    if n == 0 and g == "S":
                        empty(rotate(out[:, :], q_sb[:, t, :], t, HEADS, True), job)
                    elif n == 0:
                        empty(dve.tensor_copy(q_sb[:, t, :].rearrange("p (b a d) -> p a b d", a=2, d=HD),
                                              out[:, :].rearrange("p (a b d) -> p a b d", a=2, d=HD)), job)
                    else:
                        if g == "S":
                            if t == 0:
                                dve.wait_ge(state_out, (l + 1) * 32)
                            link(rotate(out[:, 0:P], k_sb[:, t, :], t, KV, False))
                        else:
                            link(dve.tensor_copy(k_sb[:, t, :], out[:, 0:P]))
                        empty(dve.tensor_copy(v_sb[:, t, :], out[:, P:2 * P]), job)

                def norm_sv(g, t):
                    job = ("in", g, 3, t)
                    dve.wait_ge(emptied[BANK[job]], emptied_at(job, l))
                    layer_norm_stats(sv[:, t, :], AW)
                    link(dve.tensor_tensor(sv[:, t, :], sv[:, t, :], sg_rows[:, 0, :], ALU.mult))
                    dve.tensor_tensor(sv[:, t, :], sv[:, t, :], sg_rows[:, 1, :], ALU.add).then_inc(sv_ready, 1)
                    dve.wait_ge(sv_ready, l * TILES + (GROUPS[g][t] + 1))

                def attend(g, t):
                    k = GROUPS[g][t]
                    lo_col, hi_col = mask_cols(g, t)
                    width = hi_col - lo_col
                    for h in range(HEADS):
                        job = ("score", g, t, h)
                        out = ready(job)
                        held(dve)
                        empty(dve.tensor_tensor_reduce(probs[:, h % 2, 0:width], out[:, 0:width], mask[:, lo_col:hi_col],
                                                       HD ** -0.5, sink[:, h:h + 1], ALU.add, ALU.max,
                                                       maxs[:, k % 2, h:h + 1]), job)
                        dve.tensor_scalar(negmax[:, k % 2, h:h + 1], maxs[:, k % 2, h:h + 1], -1.0, None,
                                          ALU.mult).then_inc(probs_max, 1)
                    dve.wait_ge(probs_max, l * (TILES * HEADS) + (k + 1) * HEADS)
                    dve.tensor_tensor(esink[:], sink[:], negmax[:, k % 2, :], ALU.add).then_inc(sink_in, 1)
                    dve.wait_ge(sink_exp, l * TILES + (k + 1))
                    link(dve.tensor_tensor(den[:], esink[:], rsum[:, k % 2, :], ALU.add))
                    link(dve.reciprocal(den[:], den[:]))
                    job = ("attn", g, t)
                    out = ready(job)
                    empty(dve.tensor_tensor(q_sb[:, t, :].rearrange("p (h d) -> p h d", d=HD),
                                            out[:, :].rearrange("p (h d) -> p h d", d=HD),
                                            den[:].unsqueeze(2).to_broadcast([P, HEADS, HD]), ALU.mult), job)
                    job = ("gate", g, t)
                    out = ready(job)
                    link(dve.tensor_tensor(tmp[:].rearrange("p (s d) -> p s d", d=HD),
                                           out[:, :].rearrange("p (s d) -> p s d", d=HD),
                                           bsT[:].unsqueeze(2).to_broadcast([P, SGG, HD]), ALU.add))
                    empty(dve.tensor_tensor(su[:, t, :], su[:, t, :], tmp[:], ALU.mult), job)

                def residual(g, n, t):
                    k = GROUPS[g][t]
                    job = ("out", g, n, t)
                    out = ready(job)
                    cols = slice(n * COLS, (n + 1) * COLS)
                    empty(dve.tensor_tensor(tmp[:], out[:, :], row5[:, GATE1, cols], ALU.mult), job)
                    link(dve.scalar_tensor_tensor(x[:, k, cols], x[:, k, cols], ALPHA, tmp[:], ALU.mult, ALU.add))

                def norm_modulate(g, t):
                    k = GROUPS[g][t]
                    layer_norm_stats(x[:, k, :], D)
                    link(dve.tensor_tensor(x[:, k, :], x[:, k, :], row5[:, LN1G, :], ALU.mult))
                    link(dve.tensor_tensor(x[:, k, :], x[:, k, :], row5[:, LN1B, :], ALU.add))
                    link(dve.tensor_tensor(h2[:, k, :], x[:, k, :], row5[:, SCALE2, :], ALU.mult))
                    dve.tensor_tensor(h2[:, k, :], h2[:, k, :], row5[:, SHIFT2, :], ALU.add).then_inc(h2_ready, 1)
                    dve.wait_ge(h2_ready, l * TILES + (k + 1))

                for gi, (g, tiles) in enumerate(GROUPS.items()):
                    nt = len(tiles)
                    latent = g == "S"
                    for n in range(2):
                        for t in range(nt):
                            take_qk(g, n, t)
                            if latent:
                                prompt_rows(1)
                    dve.wait_ge(layer_in, (l + 1) * (16 * 11))
                    for t in range(nt):
                        norm_sv(g, t)
                    for t in range(nt):
                        attend(g, t)
                        if latent:
                            prompt_rows(2)
                    dve.wait_ge(rows_in, (2 * l + (gi + 1)) * 80)
                    for n in range(2):
                        for t in range(nt):
                            residual(g, n, t)
                            if n == 1:
                                norm_modulate(g, t)
                            elif latent:
                                prompt_rows(1)
                    for j in range(2 * PH):
                        half_keys(g, j)
                        if latent and j >= 4:
                            prompt_rows(1)
                    for step in range(4):
                        choose(tiles[0], 0, step)
                for k in range(1, TILES):
                    for step in range(4):
                        dot_rows(k, 4 * step, 4 * step + 4)
                        if k + 1 < TILES:
                            choose(k + 1, k, step)
                    expert_weights(k)
                    add_rows(k, 0, ITERS)
                    finish_tile(k)
                link(dve.tensor_scalar(layer_base[:], layer_base[:], float(EXPERTS), None, ALU.add))
                dve.sem_clear(vchain)


_OUTS = [((1, 128, 1024), 'float32'), ((1, 512, 1024), 'float32'),
         ((1, 2, 128, 2, 64), 'float32'), ((1, 2, 128, 2, 64), 'float32')]


def _constants():
    import numpy as np
    grid_w, axis = 64, HD // 2
    pos = np.arange(512)
    inv = (1.0 / (np.float32(10000.0) ** (np.arange(0, axis, 2, dtype=np.float32) / np.float32(axis)))).astype(np.float32)
    cos, sin = [], []
    for where in (pos // grid_w, pos % grid_w):
        ang = where.astype(np.float32)[:, None] * inv[None, :]
        cos += [np.cos(ang), np.cos(ang)]
        sin += [-np.sin(ang), np.sin(ang)]
    both = np.stack([np.concatenate(cos, 1), np.concatenate(sin, 1)]).astype(np.float32)
    both = both.reshape(2, 4, P, HD).transpose(2, 0, 1, 3).reshape(P, -1)
    return np.concatenate([both, np.tile(np.arange(TOPK, dtype=np.float32), (P, 1))], 1)


def kernel(**inputs):
    import numpy as np
    import concourse.bacc as bacc
    from concourse.bass_utils import run_bass_kernel_spmd as run

    a = {name: np.asarray(v) for name, v in inputs.items()}
    laid = {
        "x_prompt": a["x_prompt"], "x_sample": a["x_sample"], "cache_k": a["cache_k"], "cache_v": a["cache_v"],
        "cond": np.stack([a["c_ctx"], a["c"][0]]).reshape(2, DC, P).transpose(2, 1, 0),
        "w_mod": a["w_mod"],
        "b_col": a["b_mod"][:, 0:2 * D].reshape(DEPTH, 16, P).transpose(2, 0, 1),
        "b_mod": a["b_mod"],
        "w_in": a["w_in"], "sg_ln_g": a["sg_ln_g"], "sg_ln_b": a["sg_ln_b"],
        "w_sT": a["w_s"].transpose(0, 3, 1, 2), "b_sT": a["b_s"].transpose(0, 2, 1),
        "attn_sink": a["attn_sink"], "w_o": a["w_o"], "ln1_g": a["ln1_g"], "ln1_b": a["ln1_b"],
        "peer_wq": a["peer_wq"],
        "keysT": np.stack([a["peer_k1"], a["peer_k2"]], 1).transpose(0, 3, 1, 2),
        "peer_u": a["peer_u"], "peer_v": a["peer_v"], "ln2_g": a["ln2_g"], "ln2_b": a["ln2_b"],
        "consts": _constants(),
    }
    nc = bacc.Bacc("TRN2", target_bir_lowering=False, num_devices=1)
    arrays, args = {}, []
    for name, v in laid.items():
        v = np.ascontiguousarray(v)
        arrays[f"in_{name}_dram"] = v
        args.append(nc.dram_tensor(f"in_{name}_dram", v.shape, mybir.dt.from_np(v.dtype), kind="ExternalInput").ap())
    for i, (shape, dtype) in enumerate(_OUTS):
        args.append(nc.dram_tensor(f"out_{i}_dram", shape, mybir.dt.from_np(np.dtype(dtype)),
                                   kind="ExternalOutput").ap())
    build(nc, *args)
    r = run(nc, [arrays], core_ids=[0])
    return tuple(r.results[0][f"out_{i}_dram"] for i in range(len(_OUTS)))
```

```python
from contextlib import ExitStack

import concourse.bass as bass
from concourse import mybir

F32 = mybir.dt.float32
U32 = mybir.dt.uint32
ALU = mybir.AluOpType
ACT = mybir.ActivationFunctionType
AX = mybir.AxisListType

P = 128
D = 1024
DC = D // P
DEPTH = 2
TILES = 5
GROUPS = {"P": [0], "S": [1, 2, 3, 4]}
HEADS = 8
HD = 64
KV = 2
AW = HEADS * HD
SGG = 8
EXPERTS = 128 * 128
TOPK = 16
PH = 8
SLOTS = PH * TOPK
ALPHA = (2.0 * DEPTH) ** 0.25
EPS = 1e-5
NEG = -8e30
LOWEST = -3.4e38
WR = 5
MR = 6
GP = 8
GL = 16
BODY = 32
COLS = 512
IN_COLS = [(0, 512), (512, 256), (768, 512), (1280, 512)]
T_ROWS = 2 * SLOTS
STEP = 4


def blocks(t):
    return ([t - 1] if t > 0 else []) + [t, 4] + ([t + 1] if t < 3 else [])


def mask_cols(group, t):
    if group == "P":
        return P, 2 * P
    return (0 if t > 0 else P), (4 * P if t < 3 else 3 * P)


def plan_jobs():
    jobs = []
    for g, tiles in GROUPS.items():
        nt = len(tiles)
        jobs += [(("xT", g, c), f"T{c % 2}") for c in range(DC)]
        for n in range(4):
            jobs += [(("in", g, n, t), f"P{t if g == 'S' else n}") for t in range(nt)]
        if g == "S":
            jobs.append((("cT", g), "T1"))
        jobs.append((("kT", g), "T0"))
        for t in range(nt):
            jobs.append((("qT", g, t), "T1"))
            for h in range(HEADS + 1):
                if h < HEADS:
                    jobs.append((("score", g, t, h), f"P{h % 2}"))
                if h:
                    jobs.append((("pT", g, t, h - 1), f"T{(h - 1) % 2}"))
            jobs.append((("attn", g, t), "O"))
            jobs.append((("gate", g, t), "O"))
            jobs += [(("yT", g, t, half), f"T{half}") for half in range(2)]
        for n in range(2):
            jobs += [(("out", g, n, t), f"P{t if g == 'S' else n}") for t in range(nt)]
        jobs += [(("hT", g, c), f"T{c % 2}") for c in range(DC)]
        for n in range(4):
            for j in range(4):
                jobs.append((("query", g, 4 * n + j), f"P{j}"))
            for j in range(4):
                jobs.append((("keys", g, 4 * n + j), f"T{j % 2}"))
    return jobs


MOVES = (TILES - 1) * SLOTS // GL
BANK, NTH, TOTAL = {}, {}, {}
for _job, _bank in plan_jobs():
    TOTAL[_bank] = TOTAL.get(_bank, 0) + 1
    BANK[_job], NTH[_job] = _bank, TOTAL[_bank]
MOD_USES = DEPTH * 6


def full_at(job, l):
    return (MOD_USES if BANK[job][0] == "P" else 0) + l * TOTAL[BANK[job]] + NTH[job]


def emptied_at(job, l):
    return full_at(job, l) + 1


def x_at(l, tiles):
    return l * TILES + (tiles + 1)


def rounds(l, k, phase, slot, i, per=1):
    prompt = 2 * SLOTS // GP if slot < GP else 0
    layer = prompt + (TILES - 1) * T_ROWS // GL
    before = phase * SLOTS // GP if k == 0 else prompt + ((k - 1) * T_ROWS + phase * SLOTS) // GL
    return l * layer + i * per + before


def v_rounds(l, k, i, per=1):
    return l * ((TILES - 1) * SLOTS // GL) + i * per + (k - 1) * SLOTS // GL


def build(nc, x_prompt, x_sample, cache_k, cache_v, cond, w_mod, b_col, b_mod, w_in, sg_ln_g, sg_ln_b,
          w_sT, b_sT, attn_sink, w_o, ln1_g, ln1_b, peer_wq, keysT, peer_u, peer_v, ln2_g, ln2_b, consts,
          y_prompt, y_sample, state_k, state_v):
    mod_rows = nc.dram_tensor("mod_rows", (DEPTH, 2, 4, D), F32, kind="Internal").ap()
    tables = (peer_u.rearrange("l e d -> (l e) d"), peer_v.rearrange("l e d -> (l e) d"))

    def chunks(w):
        return w.rearrange("l (c p) n -> l p c n", p=P)

    with ExitStack() as ctx:
        def sb(name, shape, dt=F32):
            return ctx.enter_context(nc.sbuf_tensor(name, shape, dt))

        def sem(name):
            return ctx.enter_context(nc.semaphore(name))

        x = sb("x", [P, TILES, D])
        h2 = sb("h2", [P, TILES, D])
        area = sb("area", [P, 6 * D])
        q_sb = area[:, 0:2048].rearrange("p (t n) -> p t n", t=4)
        su = area[:, 2048:4096].rearrange("p (t n) -> p t n", t=4)
        sv = area[:, 4096:6144].rearrange("p (t n) -> p t n", t=4)
        GATE1, LN1G, LN1B, SCALE2, SHIFT2 = range(5)
        row5 = area[:, 0:5120].rearrange("p (r n) -> p r n", r=5)
        m_slots = area[:, :].rearrange("p (s c n) -> p s c n", s=MR, c=2)
        row3 = sb("row3", [P, 3, D])
        sg_rows = sb("sg_rows", [P, 2, AW])
        ring8 = sb("ring8", [P, GP, D])
        w_ring = sb("w_ring", [P, WR, 2, COLS])
        hT = sb("hT", [P, DC, 512])
        w_idle = w_ring[:, 0:4].rearrange("p s c n -> p s (c n)")
        hT_idle = hT[:, :, :].rearrange("p (s c) n -> p s (c n)", c=2)
        ring = [ring8[:, b] for b in range(GP)] + [w_idle[:, b] for b in range(4)] + [hT_idle[:, b] for b in range(4)]
        scores = area[:, :].rearrange("p (t j n) -> p t j n", t=3, j=2 * PH)
        qT = sb("qT", [P, 4, P])
        k_sb = sb("k_sb", [P, 5, P])
        v_sb = sb("v_sb", [P, 5, P])
        kT = sb("kT", [P, 5, P])
        probs = sb("probs", [P, 2, 512])
        pT = sb("pT", [P, 2, 512])
        key_ring = pT[:].rearrange("p a (j n) -> p (a j) n", n=P)
        mask = sb("mask", [P, 512])
        cst = sb("cst", [P, 2 * 4 * HD + TOPK])
        rope = cst[:, 0:2 * 4 * HD].rearrange("p (a t n) -> p a t n", a=2, t=4)
        iota = cst[:, 2 * 4 * HD:]
        wsT = sb("wsT", [P, SGG, P])
        bsT = sb("bsT", [P, SGG])
        sink = sb("sink", [P, HEADS])
        keys = sb("keys", [P, 2, P])
        best = sb("best", [P, 2 * PH, TOPK])
        best_ix = sb("best_ix", [P, 2 * PH, TOPK], U32)
        ixf = sb("ixf", [P, 2 * PH, TOPK])
        left = sb("left", [P, P])
        cand = sb("cand", [P, 4, 256])
        onehot = sb("onehot", [P, 4, TOPK, TOPK])
        top = sb("top", [P, PH, TOPK])
        pos = sb("pos", [P, PH, TOPK], U32)
        part = sb("part", [P, PH, TOPK], U32)
        hi = sb("hi", [P, PH, TOPK])
        lo = sb("lo", [P, PH, TOPK])
        r1 = sb("r1", [P, PH, TOPK])
        r2 = sb("r2", [P, PH, TOPK])
        eidx = sb("eidx", [P, 2, SLOTS], U32)
        idx_stage = sb("idx_stage", [P, BODY], U32)
        gsm = sb("gsm", [P, 2, PH, TOPK])
        gsum = sb("gsum", [P, PH])
        dots = sb("dots", [P, SLOTS])
        gel = sb("gel", [P, SLOTS])
        wexp = sb("wexp", [P, SLOTS])
        dots_now = sb("dots_now", [P, GL])
        wexp_now = sb("wexp_now", [P, GL])
        diag = sb("diag", [P, 8, P])
        tmp = sb("tmp", [P, 512])
        acc = sb("acc", [P, D])
        qh = probs
        ident = sb("ident", [P, P])
        cT = sb("cT", [P, DC, 2])
        bcol = sb("bcol", [P, DEPTH, 16])
        mcol = sb("mcol", [P, DEPTH, 16, 2])
        stats = sb("stats", [P, 2, 6])
        mv = sb("mv", [P, 2])
        rstd = sb("rstd", [P, 1])
        nr = sb("nr", [P, 3])
        guess = sb("guess", [P, 1], U32)
        negmax = sb("negmax", [P, 2, HEADS])
        maxs = sb("maxs", [P, 2, HEADS])
        rsum = sb("rsum", [P, 2, HEADS])
        esink = sb("esink", [P, HEADS])
        den = sb("den", [P, HEADS])
        layer_base = sb("layer_base", [P, 1])

        bank = {b: ctx.enter_context(nc.psum_tensor(b, [P, 512], F32))
                for b in ("P0", "P1", "P2", "P3", "T0", "T1", "O", "V")}

        full = {b: sem(f"full_{b}") for b in bank}
        emptied = {b: sem(f"emptied_{b}") for b in bank}
        const_in = sem("const_in")
        built = sem("built")
        silu_done = sem("silu_done")
        bcol_done = sem("bcol_done")
        m_full = [sem(f"m_full{i}") for i in range(MR)]
        m_used = sem("m_used")
        brow_in = sem("brow_in")
        mod_stored = sem("mod_stored")
        w_full = [sem(f"w_full{i}") for i in range(WR)]
        w_used = sem("w_used")
        layer_in = sem("layer_in")
        rows_in = sem("rows_in")
        gate2_in = sem("gate2_in")
        state_out = sem("state_out")
        sv_ready = sem("sv_ready")
        probs_max = sem("probs_max")
        probs_done = sem("probs_done")
        sink_in = sem("sink_in")
        sink_exp = sem("sink_exp")
        h2_ready = sem("h2_ready")
        top_ready = sem("top_ready")
        top_exp = sem("top_exp")
        idx_ready = sem("idx_ready")
        staged = sem("staged")
        row_full = [sem(f"row_full{i}") for i in range(GL)]
        row_used = [sem(f"row_used{i}") for i in range(GL)]
        v_used = [sem(f"v_used{i}") for i in range(GL)]
        dots_moved = sem("dots_moved")
        wexp_ready = sem("wexp_ready")
        wexp_moved = sem("wexp_moved")
        diag_full = [sem(f"diag_full{i}") for i in range(8)]
        key_used = sem("key_used")
        gelu_done = sem("gelu_done")
        x_done = sem("x_done")
        vchain = sem("vchain")
        y_out = sem("y_out")
        passed = sem("passed")

        def held(eng):
            eng.sem_inc(passed, 1)

        block = ctx.enter_context(nc.Block())

        @block.sync
        def _(sp):
            sp.dma_start(cT[:], cond).then_inc(const_in, 16)
            sp.dma_start(bcol[:], b_col).then_inc(const_in, 16)
            sp.dma_start(cst[:], consts).then_inc(const_in, 16)
            sp.dma_start(x[:, 0, :], x_prompt[0]).then_inc(const_in, 16)
            sp.dma_start(x[:, 1:5, :], x_sample[0].rearrange("(t p) d -> p t d", p=P)).then_inc(const_in, 16)
            with sp.Fori(0, DEPTH) as l:
                sp.wait_ge(emptied["P3"], l * 6 + 1)
                sp.dma_start(h2[0:2, 0:4, :], b_mod[l, 2 * D:6 * D].rearrange("(a r n) -> a r n", a=1, n=D)
                             .rearrange("a r n -> (a r) n").partition_broadcast(2)).then_inc(brow_in, 16)
                for n in range(12):
                    for q in range(4):
                        u = 4 * n + q
                        if u >= MR:
                            pn, pq = divmod(u - MR, 4)
                            if pq < 3:
                                sp.wait_ge(m_used, l * 36 + 3 * pn + pq + 1)
                            else:
                                sp.wait_ge(full["P3" if pn < 4 else f"P{pn % 4}"],
                                           l * 6 + (pn + 1 if pn < 4 else 4 + pn // 4))
                        sp.dma_start(m_slots[:, u % MR], chunks(w_mod)[l, :, 2 * q:2 * q + 2, n * COLS:(n + 1) * COLS]
                                     ).then_inc(m_full[u % MR], 16)
                for b in range(4):
                    sp.wait_ge(emptied[f"P{b}"], (l + 1) * 6 + 1)
                sp.dma_start(mod_rows[l].rearrange("a r n -> a (r n)"),
                             hT[0:2, :, :].rearrange("a c n -> a (c n)")).then_inc(mod_stored, 16)
                sp.wait_ge(mod_stored, (l + 1) * 16)
                held(sp)
            with sp.Fori(0, DEPTH) as l:
                sp.wait_ge(x_done, x_at(l, 0))
                sp.dma_start(wsT[:], w_sT[l]).then_inc(layer_in, 16)
                sp.dma_start(bsT[:], b_sT[l]).then_inc(layer_in, 16)
                sp.dma_start(keys[:], keysT[l]).then_inc(layer_in, 16)
                sp.dma_start(sink[:], attn_sink[l].partition_broadcast(P)).then_inc(layer_in, 16)
                sp.dma_start(sg_rows[:, 0, :], sg_ln_g[l].partition_broadcast(P)).then_inc(layer_in, 16)
                sp.dma_start(sg_rows[:, 1, :], sg_ln_b[l].partition_broadcast(P)).then_inc(layer_in, 16)
                sp.dma_start(k_sb[:, 4, :], cache_k[0, l].rearrange("s a d -> s (a d)")).then_inc(layer_in, 16)
                sp.dma_start(v_sb[:, 4, :], cache_v[0, l].rearrange("s a d -> s (a d)")).then_inc(layer_in, 16)
                sp.dma_start(row3[:, 0, :], mod_rows[l, 0, 3].partition_broadcast(P)).then_inc(layer_in, 16)
                sp.dma_start(row3[:, 1, :], ln2_g[l].partition_broadcast(P)).then_inc(layer_in, 16)
                sp.dma_start(row3[:, 2, :], ln2_b[l].partition_broadcast(P)).then_inc(layer_in, 16)
                use = 0
                ends = []
                wu = 0
                for gi, g in enumerate(GROUPS):
                    last = len(GROUPS[g]) - 1
                    plan = [("in", n, w_in, c0, w) for n, (c0, w) in enumerate(IN_COLS)]
                    plan += [("out", n, w_o, n * COLS, COLS) for n in range(2)]
                    plan += [("query", n, peer_wq, n * COLS, COLS) for n in range(4)]
                    for kind, n, w, c0, width in plan:
                        if kind == "query" and n == 0:
                            sp.wait_ge(full["T1"], full_at(("yT", g, last, 1), l))
                            held(sp)
                            for r, src in ((GATE1, mod_rows[l, gi, 0]), (LN1G, ln1_g[l]), (LN1B, ln1_b[l]),
                                           (SCALE2, mod_rows[l, gi, 2]), (SHIFT2, mod_rows[l, gi, 1])):
                                sp.dma_start(row5[:, r, :], src.partition_broadcast(P)).then_inc(rows_in, 16)
                        for q in range(4):
                            if use >= WR:
                                s, v = ends[use - WR]
                                sp.wait_ge(s, l * 60 + v if s is w_used else full_at(v, l))
                            sp.dma_start(w_ring[:, use % WR, :, 0:width],
                                         chunks(w)[l, :, 2 * q:2 * q + 2, c0:c0 + width]
                                         ).then_inc(w_full[use % WR], 16)
                            if q < 3:
                                wu += 1
                                ends.append((w_used, wu))
                            else:
                                job = (kind, g, 4 * n + 3) if kind == "query" else (kind, g, n, last)
                                ends.append((full[BANK[job]], job))
                            use += 1
                    if g == "P":
                        sp.wait_ge(emptied[BANK["in", "P", 1, 0]], emptied_at(("in", "P", 1, 0), l))
                        sp.dma_start(state_k[0, l].rearrange("s a d -> s (a d)"), k_sb[:, 0, :]).then_inc(state_out, 16)
                        sp.dma_start(state_v[0, l].rearrange("s a d -> s (a d)"), v_sb[:, 0, :]).then_inc(state_out, 16)
            sp.wait_ge(x_done, x_at(DEPTH, 0))
            sp.dma_start(y_prompt[0], x[:, 0, :]).then_inc(y_out, 16)
            sp.dma_start(y_sample[0].rearrange("(t p) d -> p t d", p=P), x[:, 1:5, :]).then_inc(y_out, 16)
            sp.wait_ge(y_out, 32)
            sp.wait_ge(state_out, 32 * DEPTH)

        @block.gpsimd
        def _(pool):
            pool.memset(ident[:], 0.0).then_inc(built, 1)
            pool.memset(mask[:], 0.0).then_inc(built, 1)
            pool.wait_ge(built, 2)
            pool.affine_select(out=ident[:], in_=ident[:], compare_op=ALU.not_equal, fill=1.0, base=0,
                               pattern=[[-1, P]], channel_multiplier=1).then_inc(built, 1)
            pool.affine_select(out=mask[:, 0:P], in_=mask[:, 0:P], compare_op=ALU.is_ge, fill=NEG, base=0,
                               pattern=[[1, P]], channel_multiplier=-1).then_inc(built, 1)
            pool.affine_select(out=mask[:, 3 * P:4 * P], in_=mask[:, 3 * P:4 * P], compare_op=ALU.is_ge, fill=NEG,
                               base=0, pattern=[[-1, P]], channel_multiplier=1).then_inc(built, 1)

            def fetch(l, k, phase, i):
                size = GP if k == 0 else GL
                for r in range(BODY):
                    b = r % size
                    pool.wait_ge(row_used[b], rounds(l, k, phase, b, i, BODY // size) + (r // size + 1))
                    held(pool)
                    if k:
                        past = v_rounds(l, k, i if phase else 0, BODY // size) + 1 + (r // size if phase else 0)
                        pool.wait_ge(v_used[b], past)
                        held(pool)
                    if r % 8 == 0:
                        q = k * T_ROWS + phase * SLOTS + r
                        pool.tensor_copy(idx_stage[:, r:r + 8],
                                         eidx[:, k % 2, bass.ds(i * BODY + r, 8)]).then_inc(staged, 1)
                        pool.wait_ge(staged, l * (TILES * T_ROWS // 8) + i * (BODY // 8) + (q // 8 + 1))
                        held(pool)
                    pool.indirect_dma_start(
                        out=ring[b], out_offset=None, in_=tables[phase],
                        in_offset=bass.IndirectOffsetOnAxis(ap=idx_stage[:, r:r + 1], axis=0),
                    ).then_inc(row_full[b], 16)

            with pool.Fori(0, DEPTH) as l:
                for k in range(TILES):
                    pool.wait_ge(idx_ready, l * TILES + (k + 1))
                    held(pool)
                    for phase in range(2):
                        with pool.Fori(0, SLOTS // BODY) as i:
                            fetch(l, k, phase, i)
                        if k == 1 and phase == 0:
                            pool.wait_ge(x_done, x_at(l, 1))
                            pool.dma_start(row3[:, 0, :], mod_rows[l, 1, 3].partition_broadcast(P)
                                           ).then_inc(gate2_in, 16)

        @block.tensor
        def _(pe):
            pe.wait_ge(silu_done, 1)
            with pe.Fori(0, DEPTH) as l:
                for n in range(12):
                    for q in range(4):
                        u = 4 * n + q
                        pe.wait_ge(m_full[u % MR], l * (16 * 48 // MR) + 16 * (u // MR + 1))
                        for j in range(4 if n < 4 else 1):
                            b = f"P{j if n < 4 else n % 4}"
                            if q == 0:
                                pe.wait_ge(emptied[b], l * 6 + (n + 1 if n < 4 else 4 + n // 4))
                            for c in (2 * q, 2 * q + 1):
                                if n < 4:
                                    mm = pe.matmul(bank[b][:, 0:2], m_slots[:, u % MR, c % 2, j * P:(j + 1) * P],
                                                   cT[:, c, :], start=c == 0, stop=c == DC - 1)
                                else:
                                    mm = pe.matmul(bank[b][0:2, :], cT[:, c, :], m_slots[:, u % MR, c % 2, :],
                                                   start=c == 0, stop=c == DC - 1)
                            if q == 3:
                                mm.then_inc(full[b], 1)
                        if q < 3:
                            mm.then_inc(m_used, 1)

            pe.wait_ge(built, 5)
            pe.wait_ge(mod_stored, 16 * DEPTH)
            with pe.Fori(0, DEPTH) as l:
                use = [0]

                def begin(job):
                    pe.wait_ge(emptied[BANK[job]], emptied_at(job, l) - 1)
                    return bank[BANK[job]]

                def finish(mm, job):
                    mm.then_inc(full[BANK[job]], 1)

                def taken(job):
                    pe.wait_ge(emptied[BANK[job]], emptied_at(job, l))

                def slot():
                    s = use[0] % WR
                    pe.wait_ge(w_full[s], l * (80 // WR * 16) + 16 * (use[0] // WR + 1))
                    use[0] += 1
                    return w_ring[:, s]

                def project(kind, g, n, width):
                    nt = len(GROUPS[g])
                    for q in range(4):
                        w = slot()
                        for t in range(nt):
                            job = (kind, g, n, t)
                            out = begin(job) if q == 0 else bank[BANK[job]]
                            for c in (2 * q, 2 * q + 1):
                                mm = pe.matmul(out[:, 0:width], hT[:, c, t * P:(t + 1) * P], w[:, c % 2, 0:width],
                                               start=c == 0, stop=c == DC - 1)
                            if q == 3:
                                finish(mm, job)
                        if q < 3:
                            mm.then_inc(w_used, 1)

                def attend(g, t):
                    job = ("qT", g, t)
                    out = begin(job)
                    for pair in range(4):
                        mm = pe.transpose(out[:, pair * P:(pair + 1) * P], q_sb[:, t, pair * P:(pair + 1) * P], ident[:])
                    finish(mm, job)
                    taken(job)
                    keyb = blocks(t) if g == "S" else [0]
                    ao = begin(("attn", g, t))
                    heads = (GROUPS[g][0] + t) * HEADS
                    for h in range(HEADS + 2):
                        if h < HEADS:
                            job = ("score", g, t, h)
                            out = begin(job)
                            a = HD * (h // 4)
                            for i, kb in enumerate(keyb):
                                mm = pe.matmul(out[:, i * P:(i + 1) * P], qT[a:a + HD, h % 4, :], kT[a:a + HD, kb, :],
                                               start=True, stop=True)
                            finish(mm, job)
                        if 0 < h <= HEADS:
                            hh = h - 1
                            job = ("pT", g, t, hh)
                            out = begin(job)
                            pe.wait_ge(probs_done, l * (TILES * HEADS) + (heads + hh + 1))
                            for i in range(len(keyb)):
                                mm = pe.transpose(out[:, i * P:(i + 1) * P], probs[:, hh % 2, i * P:(i + 1) * P], ident[:])
                            finish(mm, job)
                        if h > 1:
                            hh = h - 2
                            taken(("pT", g, t, hh))
                            a = HD * (hh // 4)
                            for i, kb in enumerate(keyb):
                                mm = pe.matmul(ao[:, hh * HD:(hh + 1) * HD], pT[:, hh % 2, i * P:(i + 1) * P],
                                               v_sb[:, kb, a:a + HD], start=i == 0, stop=i == len(keyb) - 1)
                    finish(mm, ("attn", g, t))

                for g, tiles in GROUPS.items():
                    nt = len(tiles)
                    if g == "P":
                        pe.wait_ge(x_done, x_at(l, 0))
                        pe.wait_ge(const_in, 16 * 5)
                    for c in range(DC):
                        job = ("xT", g, c)
                        out = begin(job)
                        for t, k in enumerate(tiles):
                            mm = pe.transpose(out[:, t * P:(t + 1) * P], x[:, k, c * P:(c + 1) * P], ident[:])
                        finish(mm, job)
                    taken(("xT", g, DC - 2))
                    taken(("xT", g, DC - 1))
                    for n, (_, width) in enumerate(IN_COLS):
                        project("in", g, n, width)
                    pe.wait_ge(layer_in, (l + 1) * (16 * 11))
                    if g == "S":
                        job = ("cT", g)
                        finish(pe.transpose(begin(job)[:, 0:P], k_sb[:, 4, :], ident[:]), job)
                        taken(job)
                    job = ("kT", g)
                    out = begin(job)
                    for t in range(nt):
                        taken(("in", g, 1, t))
                        mm = pe.transpose(out[:, t * P:(t + 1) * P], k_sb[:, t, :], ident[:])
                    finish(mm, job)
                    taken(job)
                    for t in range(nt):
                        attend(g, t)
                        job = ("gate", g, t)
                        out = begin(job)
                        pe.wait_ge(sv_ready, l * TILES + (tiles[t] + 1))
                        for s in range(SGG):
                            mm = pe.matmul(out[:, s * HD:(s + 1) * HD], wsT[:, s, :], sv[:, t, s * HD:(s + 1) * HD],
                                           start=True, stop=True)
                        finish(mm, job)
                        taken(job)
                        for half, src in ((0, q_sb), (1, su)):
                            job = ("yT", g, t, half)
                            out = begin(job)
                            for c in range(4):
                                mm = pe.transpose(out[:, c * P:(c + 1) * P], src[:, t, c * P:(c + 1) * P], ident[:])
                            finish(mm, job)
                    taken(("yT", g, nt - 1, 0))
                    taken(("yT", g, nt - 1, 1))
                    for n in range(2):
                        project("out", g, n, COLS)
                    pe.wait_ge(h2_ready, l * TILES + (tiles[-1] + 1))
                    for c in range(DC):
                        job = ("hT", g, c)
                        out = begin(job)
                        for t, k in enumerate(tiles):
                            mm = pe.transpose(out[:, t * P:(t + 1) * P], h2[:, k, c * P:(c + 1) * P], ident[:])
                        finish(mm, job)
                    taken(("hT", g, DC - 2))
                    taken(("hT", g, DC - 1))
                    for n in range(4):
                        for q in range(4):
                            w = slot()
                            for j in range(4):
                                job = ("query", g, 4 * n + j)
                                out = begin(job) if q == 0 else bank[BANK[job]]
                                for c in (2 * q, 2 * q + 1):
                                    mm = pe.matmul(out[:, 0:nt * P], w[:, c % 2, j * P:(j + 1) * P], hT[:, c, 0:nt * P],
                                                   start=c == 0, stop=c == DC - 1)
                                if q == 3:
                                    finish(mm, job)
                            if q < 3:
                                mm.then_inc(w_used, 1)
                        for j in range(4):
                            job = ("keys", g, 4 * n + j)
                            out = begin(job)
                            taken(("query", g, 4 * n + j))
                            for t in range(nt):
                                mm = pe.matmul(out[:, t * P:(t + 1) * P], qh[:, j % 2, t * P:(t + 1) * P],
                                               keys[:, j % 2, :], start=True, stop=True)
                            finish(mm, job)

                for k in range(1, TILES):
                    pe.wait_ge(emptied["V"], l * (TILES - 1) + k)
                    none = mask[:, P:2 * P]
                    pe.matmul(bank["V"][:, :], none, mask[:, 0:COLS], start=True, stop=False)
                    with pe.Fori(0, SLOTS // GL) as i:
                        for b in range(GL):
                            pe.wait_ge(row_full[b], rounds(l, k, 1, b, i) * 16 + 16)
                            pe.wait_ge(diag_full[b % 8], v_rounds(l, k, i) * 2 + (b // 8 + 1))
                            pe.matmul(bank["V"][:, :], diag[:, b % 8, :], ring[b][:, 512:1024],
                                      start=False, stop=False).then_inc(v_used[b], 1)
                    pe.matmul(bank["V"][:, :], none, mask[:, 0:COLS], start=False, stop=True).then_inc(full["V"], 1)

        @block.scalar
        def _(act):
            act.wait_ge(const_in, 16 * 5)
            act.activation(cT[:], cT[:], ACT.Silu).then_inc(silu_done, 1)
            act.wait_ge(bcol_done, 1)
            with act.Fori(0, DEPTH) as l:
                for n in range(4):
                    for j in range(4):
                        act.wait_ge(full[f"P{j}"], l * 6 + (n + 1))
                        act.activation(mcol[:, bass.ds(l, 1), 4 * n + j, :].rearrange("p a c -> p (a c)"),
                                       bank[f"P{j}"][:, 0:2], ACT.Identity,
                                       bias=bcol[:, bass.ds(l, 1), 4 * n + j]
                                       ).then_inc(emptied[f"P{j}"], 1)

            with act.Fori(0, DEPTH) as l:
                def ready(job):
                    act.wait_ge(full[BANK[job]], full_at(job, l))
                    return bank[BANK[job]]

                def attend(g, t):
                    k = GROUPS[g][t]
                    job = ("qT", g, t)
                    act.activation(qT[:].rearrange("p a n -> p (a n)"), ready(job)[:, :], ACT.Copy
                                   ).then_inc(emptied[BANK[job]], 1)
                    lo_col, hi_col = mask_cols(g, t)
                    width = hi_col - lo_col
                    for h in range(HEADS + 1):
                        if h < HEADS:
                            n = k * HEADS + h
                            act.wait_ge(probs_max, l * (TILES * HEADS) + (n + 1))
                            act.activation(probs[:, h % 2, 0:width], probs[:, h % 2, 0:width], ACT.Exp,
                                           bias=negmax[:, k % 2, h:h + 1], accum_out=rsum[:, k % 2, h:h + 1]
                                           ).then_inc(probs_done, 1)
                        if h:
                            job = ("pT", g, t, h - 1)
                            act.activation(pT[:, (h - 1) % 2, 0:width], ready(job)[:, 0:width], ACT.Copy
                                           ).then_inc(emptied[BANK[job]], 1)
                    act.wait_ge(sink_in, l * TILES + (k + 1))
                    act.activation(esink[:], esink[:], ACT.Exp).then_inc(sink_exp, 1)

                def top_softmax(k):
                    act.wait_ge(top_ready, l * TILES + (k + 1))
                    act.activation(gsm[:, k % 2], gsm[:, k % 2], ACT.Exp).then_inc(top_exp, 1)

                def gelu_dots(k):
                    if k:
                        act.wait_ge(dots_moved, l * MOVES + k * SLOTS // GL)
                    else:
                        act.wait_ge(row_used[GP - 1], rounds(l, 0, 0, GP - 1, SLOTS // GP - 1) + 2)
                    act.activation(gel[:], dots[:], ACT.Gelu_apprx_tanh).then_inc(gelu_done, 1)

                def diagonals(k):
                    act.wait_ge(wexp_ready, l * TILES + (k + 1))
                    held(act)
                    with act.Fori(0, SLOTS // GL) as i:
                        for b in range(GL):
                            act.wait_ge(v_used[(b + 8) % GL], v_rounds(l, k, i) + (1 if b < 8 else 2))
                            act.activation(diag[:, b % 8, :], ident[:], ACT.Copy,
                                           scale=wexp[:, bass.ds(i * GL + b, 1)]).then_inc(diag_full[b % 8], 1)

                for gi, (g, tiles) in enumerate(GROUPS.items()):
                    nt = len(tiles)
                    for c in range(DC):
                        job = ("xT", g, c)
                        act.activation(hT[:, c, 0:nt * P], ready(job)[:, 0:nt * P], ACT.Identity,
                                       scale=mcol[:, bass.ds(l, 1), 8 + c, gi],
                                       bias=mcol[:, bass.ds(l, 1), c, gi]).then_inc(emptied[BANK[job]], 1)
                    for n, dst in ((2, su), (3, sv)):
                        for t in range(nt):
                            job = ("in", g, n, t)
                            act.activation(dst[:, t, :], ready(job)[:, :], ACT.Gelu_apprx_tanh
                                           ).then_inc(emptied[BANK[job]], 1)
                    if g == "S":
                        job = ("cT", g)
                        act.activation(kT[:, 4, :], ready(job)[:, 0:P], ACT.Copy).then_inc(emptied[BANK[job]], 1)
                    job = ("kT", g)
                    act.activation(kT[:, 0:nt, :].rearrange("p t n -> p (t n)"), ready(job)[:, 0:nt * P], ACT.Copy
                                   ).then_inc(emptied[BANK[job]], 1)
                    for t in range(nt):
                        if g == "S" and t == 1:
                            gelu_dots(0)
                        attend(g, t)
                        for half in range(2):
                            job = ("yT", g, t, half)
                            act.activation(hT[:, 4 * half:4 * half + 4, t * P:(t + 1) * P],
                                           ready(job)[:, :].rearrange("p (c n) -> p c n", c=4), ACT.Copy
                                           ).then_inc(emptied[BANK[job]], 1)
                    for c in range(DC):
                        job = ("hT", g, c)
                        act.activation(hT[:, c, 0:nt * P], ready(job)[:, 0:nt * P], ACT.Copy
                                       ).then_inc(emptied[BANK[job]], 1)
                    for j in range(2 * PH + 1):
                        if j < 2 * PH:
                            job = ("query", g, j)
                            act.activation(qh[:, j % 2, 0:nt * P], ready(job)[:, 0:nt * P], ACT.Copy
                                           ).then_inc(emptied[BANK[job]], 1)
                        if j:
                            job = ("keys", g, j - 1)
                            src = ready(job)
                            if g == "S":
                                act.activation(scores[:, :, j - 1, :], src[:, P:4 * P].rearrange("p (t n) -> p t n", n=P),
                                               ACT.Copy)
                            if j > 8:
                                act.wait_ge(key_used, l * (4 * PH) + (gi * 2 * PH + j - 8))
                            act.activation(key_ring[:, (j - 1) % 8, :], src[:, 0:P], ACT.Copy
                                           ).then_inc(emptied[BANK[job]], 1)
                    top_softmax(tiles[0])
                for k in range(1, TILES):
                    if k + 1 < TILES:
                        top_softmax(k + 1)
                    gelu_dots(k)
                    diagonals(k)

        @block.vector
        def _(dve):
            for b in bank:
                dve.sem_inc(emptied[b], 1)
            for s in row_used + v_used:
                dve.sem_inc(s, 1)
            dve.sem_inc(x_done, 1)
            dve.memset(layer_base[:], 0.0).then_inc(vchain, 1)
            dve.wait_ge(vchain, 1)
            dve.sem_clear(vchain)
            dve.wait_ge(const_in, 16 * 5)
            dve.tensor_scalar(bcol[:, :, 8:16], bcol[:, :, 8:16], 1.0, None, ALU.add).then_inc(bcol_done, 1)
            with dve.Fori(0, DEPTH) as l:
                dve.wait_ge(brow_in, (l + 1) * 16)
                for n in range(4, 12):
                    b = f"P{n % 4}"
                    dve.wait_ge(full[b], l * 6 + (4 + n // 4))
                    row, col = divmod((n - 4) * COLS, D)
                    dve.scalar_tensor_tensor(hT[0:2, n - 4, :], bank[b][0:2, :], 1.0 if row == 2 else 0.0,
                                             h2[0:2, row, col:col + COLS], ALU.add, ALU.add
                                             ).then_inc(emptied[b], 1)

            with dve.Fori(0, DEPTH) as l:
                chain = [0]

                def link(ins):
                    chain[0] += 1
                    ins.then_inc(vchain, 1)
                    dve.wait_ge(vchain, chain[0])

                def ready(job):
                    dve.wait_ge(full[BANK[job]], full_at(job, l))
                    return bank[BANK[job]]

                def empty(ins, job):
                    ins.then_inc(emptied[BANK[job]], 1)
                    dve.wait_ge(emptied[BANK[job]], emptied_at(job, l))

                def layer_norm_stats(src, width):
                    n = width // 512
                    for i in range(n):
                        link(dve.bn_stats(stats[:, i, :], src[:, i * 512:(i + 1) * 512]))
                    link(dve.bn_aggr(mv[:], stats[:, 0:n, :]))
                    link(dve.tensor_scalar(nr[:, 0:1], mv[:, 1:2], EPS, None, ALU.add))
                    link(dve.tensor_scalar(nr[:, 1:2], nr[:, 0:1], -0.5, None, ALU.mult))
                    link(dve.tensor_single_scalar(guess[:], nr[:, 0:1].bitcast(U32), 1, ALU.logical_shift_right))
                    link(dve.tensor_scalar(rstd[:].bitcast(U32), guess[:], -1.0, float(0x5f3759df), ALU.mult, ALU.add))
                    for _ in range(3):
                        link(dve.scalar_tensor_tensor(nr[:, 2:3], rstd[:], nr[:, 1:2], rstd[:], ALU.mult, ALU.mult))
                        link(dve.scalar_tensor_tensor(rstd[:], nr[:, 2:3], 1.5, rstd[:], ALU.add, ALU.mult))
                    link(dve.tensor_scalar(src, src, mv[:, 0:1], rstd[:, 0:1], ALU.subtract, ALU.mult))

                def now(k, phase, b, i):
                    return rounds(l, k, phase, b, i) + 2

                def dot_rows(k, i0, i1):
                    held(dve)
                    with dve.Fori(i0, i1) as i:
                        for b in range(GL):
                            dve.wait_ge(row_full[b], rounds(l, k, 0, b, i) * 16 + 16)
                            dve.scalar_tensor_tensor(ring[b], ring[b], 1.0, h2[:, k, :], ALU.mult, ALU.mult,
                                                     accum_out=dots_now[:, b:b + 1]).then_inc(row_used[b], 1)
                        dve.wait_ge(row_used[GL - 1], now(k, 0, GL - 1, i))
                        dve.tensor_copy(dots[:, bass.ds(i * GL, GL)], dots_now[:, :]).then_inc(dots_moved, 1)
                        dve.wait_ge(dots_moved, l * MOVES + i + ((k - 1) * SLOTS // GL + 1))
                        held(dve)

                def sum_of(k):
                    return h2[:, k, :] if k else acc[:]

                def expert_weights(k):
                    dve.wait_ge(gelu_done, l * TILES + (k + 1))
                    dve.tensor_tensor(wexp[:], gel[:], gsm[:, k % 2].rearrange("p h j -> p (h j)"), ALU.mult
                                      ).then_inc(wexp_ready, 1)
                    link(dve.memset(sum_of(k), 0.0))
                    dve.wait_ge(wexp_ready, l * TILES + (k + 1))

                def add_rows(k, i0, i1):
                    held(dve)
                    with dve.Fori(i0, i1) as i:
                        dve.tensor_copy(wexp_now[:, :], wexp[:, bass.ds(i * GL, GL)]).then_inc(wexp_moved, 1)
                        dve.wait_ge(wexp_moved, l * MOVES + i + ((k - 1) * SLOTS // GL + 1))
                        for b in range(GL):
                            dve.wait_ge(row_full[b], rounds(l, k, 1, b, i) * 16 + 16)
                            if b:
                                dve.wait_ge(row_used[b - 1], now(k, 1, b - 1, i))
                            dve.scalar_tensor_tensor(h2[:, k, 0:512], ring[b][:, 0:512], wexp_now[:, b:b + 1],
                                                     h2[:, k, 0:512], ALU.mult, ALU.add).then_inc(row_used[b], 1)
                        dve.wait_ge(row_used[GL - 1], now(k, 1, GL - 1, i))
                        held(dve)

                def gate_sum(k):
                    total = sum_of(k)
                    if k == 1:
                        dve.wait_ge(gate2_in, (l + 1) * 16)
                    if k == 0:
                        link(dve.tensor_tensor(total, total, row3[:, 0, :], ALU.mult))
                    else:
                        link(dve.tensor_tensor(total[:, 0:512], total[:, 0:512], row3[:, 0, 0:512], ALU.mult))
                        dve.wait_ge(full["V"], l * (TILES - 1) + k)
                        dve.tensor_tensor(total[:, 512:1024], bank["V"][:, :], row3[:, 0, 512:1024], ALU.mult
                                          ).then_inc(emptied["V"], 1)
                        dve.wait_ge(emptied["V"], l * (TILES - 1) + (k + 1))

                def finish_tile(k):
                    link(dve.scalar_tensor_tensor(x[:, k, :], x[:, k, :], ALPHA, sum_of(k), ALU.mult, ALU.add))
                    layer_norm_stats(x[:, k, :], D)
                    link(dve.tensor_tensor(x[:, k, :], x[:, k, :], row3[:, 1, :], ALU.mult))
                    dve.tensor_tensor(x[:, k, :], x[:, k, :], row3[:, 2, :], ALU.add).then_inc(x_done, 1)
                    dve.wait_ge(x_done, x_at(l, k + 1))

                prompt_row = [0]

                def prompt_rows(steps):
                    for _ in range(steps * STEP):
                        phase, row = divmod(prompt_row[0], SLOTS)
                        if prompt_row[0] == SLOTS:
                            expert_weights(0)
                        i, b = divmod(row, GP)
                        dve.wait_ge(row_full[b], rounds(l, 0, phase, b, i) * 16 + 16)
                        if phase == 0:
                            dve.scalar_tensor_tensor(ring[b], ring[b], 1.0, h2[:, 0, :], ALU.mult, ALU.mult,
                                                     accum_out=dots[:, row:row + 1]).then_inc(row_used[b], 1)
                        else:
                            if row:
                                before = divmod(row - 1, GP)
                                dve.wait_ge(row_used[before[1]], now(0, 1, before[1], before[0]))
                            dve.scalar_tensor_tensor(acc[:], ring[b], wexp[:, row:row + 1], acc[:], ALU.mult,
                                                     ALU.add).then_inc(row_used[b], 1)
                        prompt_row[0] += 1
                    dve.wait_ge(row_used[b], now(0, phase, b, i))
                    held(dve)
                    if prompt_row[0] == 2 * SLOTS:
                        gate_sum(0)
                        finish_tile(0)

                def half_keys(j, s, done):
                    link(dve.max(best[:, j, 0:8], s))
                    link(dve.max_index(best_ix[:, j, 0:8], best[:, j, 0:8], s))
                    ins = dve.match_replace(left[:], best[:, j, 0:8], s, LOWEST)
                    if done is None:
                        link(ins)
                    else:
                        ins.then_inc(key_used, 1)
                        dve.wait_ge(key_used, done)
                        held(dve)
                    link(dve.max(best[:, j, 8:16], left[:]))
                    link(dve.max_index(best_ix[:, j, 8:16], best[:, j, 8:16], left[:]))

                def first_tile_keys(g, j):
                    job = ("keys", g, j)
                    dve.wait_ge(emptied[BANK[job]], emptied_at(job, l))
                    held(dve)
                    gi = list(GROUPS).index(g)
                    half_keys(j, key_ring[:, j % 8, :], l * (4 * PH) + (gi * 2 * PH + j + 1))

                def best_pairs(half):
                    pair = best[:].rearrange("p (h a) j -> p h a j", a=2)[:, 4 * half:4 * half + 4]
                    link(dve.tensor_tensor(cand[:].rearrange("p h (i j) -> p h i j", i=TOPK),
                                           pair[:, :, 0, :].unsqueeze(3).to_broadcast([P, 4, TOPK, TOPK]),
                                           pair[:, :, 1, :].unsqueeze(2).to_broadcast([P, 4, TOPK, TOPK]), ALU.add))
                    for i in range(4):
                        h = 4 * half + i
                        link(dve.max(top[:, h, 0:8], cand[:, i, :]))
                        link(dve.max_index(pos[:, h, 0:8], top[:, h, 0:8], cand[:, i, :]))
                        link(dve.match_replace(cand[:, i, :], top[:, h, 0:8], cand[:, i, :], LOWEST))
                        link(dve.max(top[:, h, 8:16], cand[:, i, :]))
                        link(dve.max_index(pos[:, h, 8:16], top[:, h, 8:16], cand[:, i, :]))

                def softmax_in(k):
                    dve.tensor_tensor(gsm[:, k % 2], top[:], top[:, :, 0:1].to_broadcast([P, PH, TOPK]),
                                      ALU.subtract).then_inc(top_ready, 1)

                def split_positions(half):
                    hs, js = slice(4 * half, 4 * half + 4), slice(8 * half, 8 * half + 8)
                    link(dve.tensor_copy(ixf[:, js, :], best_ix[:, js, :]))
                    link(dve.tensor_single_scalar(part[:, hs, :], pos[:, hs, :], 4, ALU.logical_shift_right))
                    link(dve.tensor_copy(hi[:, hs, :], part[:, hs, :]))
                    link(dve.tensor_single_scalar(part[:, hs, :], pos[:, hs, :], 15, ALU.bitwise_and))
                    link(dve.tensor_copy(lo[:, hs, :], part[:, hs, :]))

                def pick(half, which):
                    src, dst = ((hi, r1), (lo, r2))[which]
                    hs = slice(4 * half, 4 * half + 4)
                    shape = [P, 4, TOPK, TOPK]
                    num = ixf[:].rearrange("p (h a) j -> p h a j", a=2)[:, hs, which, :]
                    link(dve.tensor_tensor(onehot[:], src[:, hs, :].unsqueeze(3).to_broadcast(shape),
                                           iota.unsqueeze(1).unsqueeze(1).to_broadcast(shape), ALU.is_equal))
                    link(dve.tensor_tensor(onehot[:], onehot[:], num.unsqueeze(2).to_broadcast(shape), ALU.mult))
                    link(dve.tensor_reduce(dst[:, hs, :], onehot[:], AX.X, ALU.add))

                def expert_numbers(k):
                    link(dve.scalar_tensor_tensor(r1[:], r1[:], 128.0, r2[:], ALU.mult, ALU.add))
                    dve.tensor_scalar(eidx[:, k % 2, :].rearrange("p (h j) -> p h j", h=PH), r1[:],
                                      layer_base[:, 0:1], None, ALU.add).then_inc(idx_ready, 1)
                    dve.wait_ge(top_exp, l * TILES + (k + 1))
                    link(dve.tensor_reduce(gsum[:], gsm[:, k % 2], AX.X, ALU.add))
                    link(dve.reciprocal(gsum[:], gsum[:]))
                    link(dve.tensor_tensor(gsm[:, k % 2], gsm[:, k % 2],
                                           gsum[:].unsqueeze(2).to_broadcast([P, PH, TOPK]), ALU.mult))
                    dve.wait_ge(idx_ready, l * TILES + (k + 1))

                def choose(k, step):
                    if step == 0:
                        best_pairs(0)
                    elif step == 1:
                        best_pairs(1)
                        softmax_in(k)
                    elif step == 2:
                        split_positions(0)
                        split_positions(1)
                        pick(0, 0)
                    elif step == 3:
                        pick(0, 1)
                        pick(1, 0)
                    elif step == 4:
                        pick(1, 1)
                    else:
                        expert_numbers(k)

                def rotate(src, dst, t, nh, perm):
                    n = nh * HD
                    c, s = rope[:, 0, t, :], rope[:, 1, t, :]
                    if perm:
                        v = src.rearrange("p (a b d) -> p a b d", a=2, d=HD)
                        shape = [P, 2, 4, HD]
                        o = dst.rearrange("p (b a d) -> p a b d", a=2, d=HD)
                        cb = c.unsqueeze(1).unsqueeze(1).to_broadcast(shape)
                        swapped = tmp[:, 0:n].rearrange("p (a b d) -> p a b d", a=2, d=HD)
                    else:
                        v = src.rearrange("p (a d) -> p a d", d=HD)
                        shape = [P, nh, HD]
                        o = dst.rearrange("p (a d) -> p a d", d=HD)
                        cb = c.unsqueeze(1).to_broadcast(shape)
                        swapped = tmp[:, 0:n].rearrange("p (a d) -> p a d", d=HD)
                    link(dve.tensor_tensor(o, v, cb, ALU.mult))
                    x4 = src.rearrange("p (a e f) -> p a e f", e=4, f=16)
                    y4 = tmp[:, 0:n].rearrange("p (a e f) -> p a e f", e=4, f=16)
                    s4 = s.rearrange("p (e f) -> p e f", e=4)
                    for z in range(2):
                        link(dve.tensor_tensor(y4[:, :, z::2, :], x4[:, :, 1 - z::2, :],
                                               s4[:, z::2, :].unsqueeze(1).to_broadcast([P, nh, 2, 16]), ALU.mult))
                    return dve.tensor_tensor(o, o, swapped, ALU.add)

                def take_qk(g, n, t):
                    job = ("in", g, n, t)
                    out = ready(job)
                    if n == 0 and g == "S":
                        empty(rotate(out[:, :], q_sb[:, t, :], t, HEADS, True), job)
                    elif n == 0:
                        empty(dve.tensor_copy(q_sb[:, t, :].rearrange("p (b a d) -> p a b d", a=2, d=HD),
                                              out[:, :].rearrange("p (a b d) -> p a b d", a=2, d=HD)), job)
                    else:
                        if g == "S":
                            if t == 0:
                                dve.wait_ge(state_out, (l + 1) * 32)
                            link(rotate(out[:, 0:P], k_sb[:, t, :], t, KV, False))
                        else:
                            link(dve.tensor_copy(k_sb[:, t, :], out[:, 0:P]))
                        empty(dve.tensor_copy(v_sb[:, t, :], out[:, P:2 * P]), job)

                def norm_sv(g, t):
                    job = ("in", g, 3, t)
                    dve.wait_ge(emptied[BANK[job]], emptied_at(job, l))
                    layer_norm_stats(sv[:, t, :], AW)
                    link(dve.tensor_tensor(sv[:, t, :], sv[:, t, :], sg_rows[:, 0, :], ALU.mult))
                    dve.tensor_tensor(sv[:, t, :], sv[:, t, :], sg_rows[:, 1, :], ALU.add).then_inc(sv_ready, 1)
                    dve.wait_ge(sv_ready, l * TILES + (GROUPS[g][t] + 1))

                def attend(g, t):
                    k = GROUPS[g][t]
                    lo_col, hi_col = mask_cols(g, t)
                    width = hi_col - lo_col
                    for h in range(HEADS):
                        job = ("score", g, t, h)
                        out = ready(job)
                        held(dve)
                        empty(dve.tensor_tensor_reduce(probs[:, h % 2, 0:width], out[:, 0:width], mask[:, lo_col:hi_col],
                                                       HD ** -0.5, sink[:, h:h + 1], ALU.add, ALU.max,
                                                       maxs[:, k % 2, h:h + 1]), job)
                        dve.tensor_scalar(negmax[:, k % 2, h:h + 1], maxs[:, k % 2, h:h + 1], -1.0, None,
                                          ALU.mult).then_inc(probs_max, 1)
                        if g == "S":
                            prompt_rows(1)
                    dve.wait_ge(probs_max, l * (TILES * HEADS) + (k + 1) * HEADS)
                    dve.tensor_tensor(esink[:], sink[:], negmax[:, k % 2, :], ALU.add).then_inc(sink_in, 1)
                    dve.wait_ge(sink_exp, l * TILES + (k + 1))
                    link(dve.tensor_tensor(den[:], esink[:], rsum[:, k % 2, :], ALU.add))
                    link(dve.reciprocal(den[:], den[:]))
                    job = ("attn", g, t)
                    out = ready(job)
                    empty(dve.tensor_tensor(q_sb[:, t, :].rearrange("p (h d) -> p h d", d=HD),
                                            out[:, :].rearrange("p (h d) -> p h d", d=HD),
                                            den[:].unsqueeze(2).to_broadcast([P, HEADS, HD]), ALU.mult), job)
                    job = ("gate", g, t)
                    out = ready(job)
                    link(dve.tensor_tensor(tmp[:].rearrange("p (s d) -> p s d", d=HD),
                                           out[:, :].rearrange("p (s d) -> p s d", d=HD),
                                           bsT[:].unsqueeze(2).to_broadcast([P, SGG, HD]), ALU.add))
                    empty(dve.tensor_tensor(su[:, t, :], su[:, t, :], tmp[:], ALU.mult), job)

                def residual(g, n, t):
                    k = GROUPS[g][t]
                    job = ("out", g, n, t)
                    out = ready(job)
                    cols = slice(n * COLS, (n + 1) * COLS)
                    empty(dve.tensor_tensor(tmp[:], out[:, :], row5[:, GATE1, cols], ALU.mult), job)
                    link(dve.scalar_tensor_tensor(x[:, k, cols], x[:, k, cols], ALPHA, tmp[:], ALU.mult, ALU.add))

                def norm_modulate(g, t):
                    k = GROUPS[g][t]
                    layer_norm_stats(x[:, k, :], D)
                    link(dve.tensor_tensor(x[:, k, :], x[:, k, :], row5[:, LN1G, :], ALU.mult))
                    link(dve.tensor_tensor(x[:, k, :], x[:, k, :], row5[:, LN1B, :], ALU.add))
                    link(dve.tensor_tensor(h2[:, k, :], x[:, k, :], row5[:, SCALE2, :], ALU.mult))
                    dve.tensor_tensor(h2[:, k, :], h2[:, k, :], row5[:, SHIFT2, :], ALU.add).then_inc(h2_ready, 1)
                    dve.wait_ge(h2_ready, l * TILES + (k + 1))

                for gi, (g, tiles) in enumerate(GROUPS.items()):
                    nt = len(tiles)
                    latent = g == "S"
                    for n in range(2):
                        for t in range(nt):
                            take_qk(g, n, t)
                            if latent:
                                prompt_rows(2 - n)
                    dve.wait_ge(layer_in, (l + 1) * (16 * 11))
                    if latent:
                        prompt_rows(8)
                    for t in range(nt):
                        norm_sv(g, t)
                        if latent:
                            prompt_rows(1)
                    for t in range(nt):
                        attend(g, t)
                    if latent:
                        prompt_rows(4)
                    dve.wait_ge(rows_in, (2 * l + (gi + 1)) * 80)
                    for n in range(2):
                        for t in range(nt):
                            residual(g, n, t)
                            if n == 1:
                                norm_modulate(g, t)
                    if latent:
                        prompt_rows(4)
                    for j in range(2 * PH):
                        first_tile_keys(g, j)
                        if j == PH - 1:
                            best_pairs(0)
                            split_positions(0)
                            pick(0, 0)
                            pick(0, 1)
                    best_pairs(1)
                    softmax_in(tiles[0])
                    split_positions(1)
                    pick(1, 0)
                    pick(1, 1)
                    expert_numbers(tiles[0])
                for k in range(1, TILES):
                    choosing = k + 1 < TILES
                    for i in range(SLOTS // GL):
                        dot_rows(k, i, i + 1)
                        if choosing:
                            for j in range(3 * i, min(3 * i + 3, 2 * PH)):
                                half_keys(j, scores[:, k - 1, j, :], None)
                            if i >= 6:
                                choose(k + 1, i - 6)
                    expert_weights(k)
                    for i in range(SLOTS // GL):
                        add_rows(k, i, i + 1)
                        if choosing and i < 4:
                            choose(k + 1, i + 2)
                        if k > 1 and i == 4:
                            finish_tile(k - 1)
                    gate_sum(k)
                finish_tile(TILES - 1)
                link(dve.tensor_scalar(layer_base[:], layer_base[:], float(EXPERTS), None, ALU.add))
                dve.sem_clear(vchain)


_OUTS = [((1, 128, 1024), 'float32'), ((1, 512, 1024), 'float32'),
         ((1, 2, 128, 2, 64), 'float32'), ((1, 2, 128, 2, 64), 'float32')]


def _constants():
    import numpy as np
    grid_w, axis = 64, HD // 2
    pos = np.arange(512)
    inv = (1.0 / (np.float32(10000.0) ** (np.arange(0, axis, 2, dtype=np.float32) / np.float32(axis)))).astype(np.float32)
    cos, sin = [], []
    for where in (pos // grid_w, pos % grid_w):
        ang = where.astype(np.float32)[:, None] * inv[None, :]
        cos += [np.cos(ang), np.cos(ang)]
        sin += [-np.sin(ang), np.sin(ang)]
    both = np.stack([np.concatenate(cos, 1), np.concatenate(sin, 1)]).astype(np.float32)
    both = both.reshape(2, 4, P, HD).transpose(2, 0, 1, 3).reshape(P, -1)
    return np.concatenate([both, np.tile(np.arange(TOPK, dtype=np.float32), (P, 1))], 1)


def kernel(**inputs):
    import numpy as np
    import concourse.bacc as bacc
    from concourse.bass_utils import run_bass_kernel_spmd as run

    a = {name: np.asarray(v) for name, v in inputs.items()}
    laid = {
        "x_prompt": a["x_prompt"], "x_sample": a["x_sample"], "cache_k": a["cache_k"], "cache_v": a["cache_v"],
        "cond": np.stack([a["c_ctx"], a["c"][0]]).reshape(2, DC, P).transpose(2, 1, 0),
        "w_mod": a["w_mod"],
        "b_col": a["b_mod"][:, 0:2 * D].reshape(DEPTH, 16, P).transpose(2, 0, 1),
        "b_mod": a["b_mod"],
        "w_in": a["w_in"], "sg_ln_g": a["sg_ln_g"], "sg_ln_b": a["sg_ln_b"],
        "w_sT": a["w_s"].transpose(0, 3, 1, 2), "b_sT": a["b_s"].transpose(0, 2, 1),
        "attn_sink": a["attn_sink"], "w_o": a["w_o"], "ln1_g": a["ln1_g"], "ln1_b": a["ln1_b"],
        "peer_wq": a["peer_wq"],
        "keysT": np.stack([a["peer_k1"], a["peer_k2"]], 1).transpose(0, 3, 1, 2),
        "peer_u": a["peer_u"], "peer_v": a["peer_v"], "ln2_g": a["ln2_g"], "ln2_b": a["ln2_b"],
        "consts": _constants(),
    }
    nc = bacc.Bacc("TRN2", target_bir_lowering=False, num_devices=1)
    arrays, args = {}, []
    for name, v in laid.items():
        v = np.ascontiguousarray(v)
        arrays[f"in_{name}_dram"] = v
        args.append(nc.dram_tensor(f"in_{name}_dram", v.shape, mybir.dt.from_np(v.dtype), kind="ExternalInput").ap())
    for i, (shape, dtype) in enumerate(_OUTS):
        args.append(nc.dram_tensor(f"out_{i}_dram", shape, mybir.dt.from_np(np.dtype(dtype)),
                                   kind="ExternalOutput").ap())
    build(nc, *args)
    r = run(nc, [arrays], core_ids=[0])
    return tuple(r.results[0][f"out_{i}_dram"] for i in range(len(_OUTS)))
```
